# Optimizing a Trainium2 kernel written in Bass

```python
import math
import jax, jax.numpy as jnp
from jax import lax
import numpy as np

D_MODEL = 1024
BATCH = 1
SEQ = 256
DEPTH = 2

EPS = 1e-6
HEAD_DIM = 64
ATT_HEADS = 4
ATT_WIDTH = ATT_HEADS * HEAD_DIM
DILATED_PATTERNS = ((128, 1), (512, 4), (2048, 16))
ATT_BLOCK = 128
REL_BUCKETS = 32
REL_MAX_DISTANCE = 2048
GLA_HEADS = 4
GLA_DK = 64
GLA_DV = 128
GLA_RANK = 16
GLA_TAU = 16.0
GLA_CHUNK = 64
CONV_CH = 256
CONV_WIDTH = 3
MIX_WIDTH = ATT_WIDTH + GLA_HEADS * GLA_DV + CONV_CH
SPLIT_SIZES = (ATT_WIDTH, ATT_WIDTH, ATT_WIDTH,
               GLA_HEADS * GLA_DK, GLA_HEADS * GLA_DK,
               GLA_HEADS * GLA_DV, GLA_HEADS * GLA_DV,
               GLA_RANK,
               CONV_CH, CONV_CH, CONV_CH)
IN_COLS = 3 * ATT_WIDTH + 2 * GLA_HEADS * GLA_DK + 2 * GLA_HEADS * GLA_DV + GLA_RANK + 3 * CONV_CH
FFN_DENSE = 2816
N_EXPERTS = 8
TOP_K = 2
FFN_EXPERT = 3584
N_DENSE = (DEPTH + 1) // 2
N_MOE = DEPTH // 2

kernel_name = "hybrid_dilated_gla_shortconv_moe"

def rmsnorm(x, g):
    xf = x.astype(jnp.float32)
    y = xf * lax.rsqrt(jnp.mean(xf * xf, axis=-1, keepdims=True) + EPS)
    return (y * g.astype(jnp.float32)).astype(x.dtype)

def rel_bucket(dist):
    max_exact = REL_BUCKETS // 2
    d = jnp.maximum(dist, 0)
    log_ratio = jnp.log(jnp.maximum(d, 1).astype(jnp.float32) / max_exact) / math.log(REL_MAX_DISTANCE / max_exact)
    large = jnp.minimum(max_exact + (log_ratio * (REL_BUCKETS - max_exact)).astype(jnp.int32), REL_BUCKETS - 1)
    return jnp.where(d < max_exact, d, large)

def dilated_branch(q, k, v, rel_bias, window, dilation):
    b, s, h, hd = q.shape
    span = window // dilation
    L = s // dilation
    nblk = -(-L // ATT_BLOCK)
    Lp = nblk * ATT_BLOCK
    pad_end = ((0, 0), (0, Lp - L), (0, 0), (0, 0), (0, 0))

    def sub(t):
        return jnp.pad(t.reshape(b, L, dilation, h, hd), pad_end)

    qs = sub(q).reshape(b, nblk, ATT_BLOCK, dilation, h, hd)
    pad_front = ((0, 0), (ATT_BLOCK, 0), (0, 0), (0, 0), (0, 0))
    kp = jnp.pad(sub(k), pad_front)
    vp = jnp.pad(sub(v), pad_front)

    def span_blocks(t):
        prev = t[:, :Lp].reshape(b, nblk, ATT_BLOCK, dilation, h, hd)
        cur = t[:, ATT_BLOCK:].reshape(b, nblk, ATT_BLOCK, dilation, h, hd)
        return jnp.concatenate([prev, cur], axis=2)

    ks = span_blocks(kp)
    vs = span_blocks(vp)
    logits = jnp.einsum('bnqrhd,bnkrhd->bnrhqk', qs, ks).astype(jnp.float32) * (hd ** -0.5)

    qi = jnp.arange(ATT_BLOCK)[:, None]
    kj = jnp.arange(2 * ATT_BLOCK)[None, :]
    sub_dist = qi - kj + ATT_BLOCK
    band = (sub_dist >= 0) & (sub_dist <= span)
    bias = jnp.transpose(rel_bias[rel_bucket(sub_dist * dilation)].astype(jnp.float32), (2, 0, 1))
    key_exists = ~((jnp.arange(nblk)[:, None, None] == 0) & (kj[None] < ATT_BLOCK))
    valid = band[None] & key_exists
    logits = jnp.where(valid[None, :, None, None], logits + bias[None, None, None], -jnp.inf)

    lse = jax.nn.logsumexp(logits, axis=-1)
    p = jnp.exp(logits - lse[..., None]).astype(v.dtype)
    o = jnp.einsum('bnrhqk,bnkrhd->bnqrhd', p, vs)
    o = o.reshape(b, Lp, dilation, h, hd)[:, :L].reshape(b, s, h, hd)
    lse = jnp.transpose(lse, (0, 1, 4, 2, 3)).reshape(b, Lp, dilation, h)[:, :L].reshape(b, s, h)
    return o, lse

def dilated_attention(q, k, v, rel_bias):
    outs, lses = [], []
    for window, dilation in DILATED_PATTERNS:
        o, lse = dilated_branch(q, k, v, rel_bias, window, dilation)
        outs.append(o)
        lses.append(lse)
    alpha = jax.nn.softmax(jnp.stack(lses, axis=0), axis=0)
    o = jnp.sum(alpha[..., None] * jnp.stack(outs, axis=0).astype(jnp.float32), axis=0)
    return o.astype(q.dtype)

def gla_mixer(q, k, v, log_a):
    b, s, h, dk = q.shape
    dv = v.shape[-1]
    n = s // GLA_CHUNK

    def chunks(t):
        return jnp.transpose(t.astype(jnp.float32).reshape(b, n, GLA_CHUNK, h, t.shape[-1]), (1, 0, 3, 2, 4))

    qc, kc, vc, ac = chunks(q * (dk ** -0.5)), chunks(k), chunks(v), chunks(log_a)
    causal = jnp.tril(jnp.ones((GLA_CHUNK, GLA_CHUNK), dtype=bool))

    def step(state, inp):
        qt, kt, vt, at = inp
        cum = jnp.cumsum(at, axis=2)
        o_inter = jnp.einsum('bhck,bhkv->bhcv', qt * jnp.exp(cum), state)
        rel = cum[:, :, :, None, :] - cum[:, :, None, :, :]
        decay = jnp.exp(jnp.where(causal[:, :, None], rel, -jnp.inf))
        scores = jnp.einsum('bhtk,bhsk,bhtsk->bhts', qt, kt, decay)
        o_intra = jnp.einsum('bhts,bhsv->bhtv', scores, vt)
        last = cum[:, :, -1:, :]
        new_state = jnp.exp(last[:, :, 0, :, None]) * state + jnp.einsum('bhck,bhcv->bhkv', kt * jnp.exp(last - cum), vt)
        return new_state, o_inter + o_intra

    state0 = jnp.zeros((b, h, dk, dv), jnp.float32)
    _, o = lax.scan(step, state0, (qc, kc, vc, ac))
    return jnp.transpose(o, (1, 0, 3, 2, 4)).reshape(b, s, h, dv)

def short_conv_mixer(h_in, gate_b, gate_c, conv_w):
    u = gate_c * h_in
    y = lax.conv_general_dilated(u, conv_w[:, None, :].astype(u.dtype), window_strides=(1,),
                                 padding=[(CONV_WIDTH - 1, 0)],
                                 dimension_numbers=('NWC', 'WIO', 'NWC'),
                                 feature_group_count=CONV_CH)
    return gate_b * y

def swiglu(h, w1, w3, w2):
    return (jax.nn.silu(h @ w1) * (h @ w3)) @ w2

def moe_swiglu(h, w_router, w1, w3, w2):
    logits = jnp.einsum('bsd,de->bse', h, w_router).astype(jnp.float32)
    top_val, top_idx = lax.top_k(logits, TOP_K)
    top_w = jax.nn.softmax(top_val, axis=-1)
    gates = jnp.sum(jax.nn.one_hot(top_idx, N_EXPERTS, dtype=jnp.float32) * top_w[..., None], axis=-2)
    out = jnp.zeros_like(h)
    for e in range(N_EXPERTS):
        out = out + gates[..., e:e + 1].astype(h.dtype) * swiglu(h, w1[e], w3[e], w2[e])
    return out

def setup_inputs(seed: int = 0) -> dict:
    key = jax.random.key(seed)
    ks = jax.random.split(key, 20)
    f32 = jnp.float32

    def nrm(k, shape, fan_in):
        return jax.random.normal(k, shape, f32) * fan_in ** -0.5

    def gain(k, shape):
        return 1.0 + 0.02 * jax.random.normal(k, shape, f32)

    return {
        "x": jax.random.normal(ks[0], (BATCH, SEQ, D_MODEL), f32),
        "w_mix_in": nrm(ks[1], (DEPTH, D_MODEL, IN_COLS), D_MODEL),
        "w_mix_out": nrm(ks[2], (DEPTH, MIX_WIDTH, D_MODEL), MIX_WIDTH),
        "g_mix": gain(ks[3], (DEPTH, D_MODEL)),
        "rel_bias": 0.2 * jax.random.normal(ks[4], (REL_BUCKETS, ATT_HEADS), f32),
        "gla_w_gate": nrm(ks[5], (DEPTH, GLA_RANK, GLA_HEADS * GLA_DK), GLA_RANK),
        "gla_b_gate": 0.1 * jax.random.normal(ks[6], (DEPTH, GLA_HEADS * GLA_DK), f32),
        "gla_g_norm": gain(ks[7], (DEPTH, GLA_DV)),
        "conv_w": nrm(ks[8], (DEPTH, CONV_WIDTH, CONV_CH), CONV_WIDTH),
        "g_ffn": gain(ks[9], (DEPTH, D_MODEL)),
        "ffn_w1": nrm(ks[10], (N_DENSE, D_MODEL, FFN_DENSE), D_MODEL),
        "ffn_w3": nrm(ks[11], (N_DENSE, D_MODEL, FFN_DENSE), D_MODEL),
        "ffn_w2": nrm(ks[12], (N_DENSE, FFN_DENSE, D_MODEL), FFN_DENSE),
        "moe_router": nrm(ks[13], (N_MOE, D_MODEL, N_EXPERTS), D_MODEL),
        "moe_w1": nrm(ks[14], (N_MOE, N_EXPERTS, D_MODEL, FFN_EXPERT), D_MODEL),
        "moe_w3": nrm(ks[15], (N_MOE, N_EXPERTS, D_MODEL, FFN_EXPERT), D_MODEL),
        "moe_w2": nrm(ks[16], (N_MOE, N_EXPERTS, FFN_EXPERT, D_MODEL), FFN_EXPERT),
        "g_final": gain(ks[17], (D_MODEL,)),
    }

def reference(x, w_mix_in, w_mix_out, g_mix, rel_bias, gla_w_gate, gla_b_gate, gla_g_norm, conv_w,
              g_ffn, ffn_w1, ffn_w3, ffn_w2, moe_router, moe_w1, moe_w3, moe_w2, g_final):
    b, s, _ = x.shape
    split_at = np.cumsum(SPLIT_SIZES)[:-1].tolist()
    for layer in range(DEPTH):
        h = rmsnorm(x, g_mix[layer])
        u = h @ w_mix_in[layer]
        (aq, ak, av, gq, gk, gv, gr, glr, c_in, c_b, c_c) = jnp.split(u, split_at, axis=-1)

        att = dilated_attention(aq.reshape(b, s, ATT_HEADS, HEAD_DIM),
                                ak.reshape(b, s, ATT_HEADS, HEAD_DIM),
                                av.reshape(b, s, ATT_HEADS, HEAD_DIM), rel_bias)
        att = att.reshape(b, s, ATT_WIDTH)

        log_a = jax.nn.log_sigmoid((glr @ gla_w_gate[layer] + gla_b_gate[layer]).astype(jnp.float32)) / GLA_TAU
        go = gla_mixer(gq.reshape(b, s, GLA_HEADS, GLA_DK), gk.reshape(b, s, GLA_HEADS, GLA_DK),
                       gv.reshape(b, s, GLA_HEADS, GLA_DV), log_a.reshape(b, s, GLA_HEADS, GLA_DK))
        go = rmsnorm(go.astype(x.dtype), gla_g_norm[layer]).reshape(b, s, GLA_HEADS * GLA_DV) * jax.nn.silu(gr)

        cv = short_conv_mixer(c_in, c_b, c_c, conv_w[layer])

        mixed = jnp.concatenate([att, go, cv], axis=-1)
        x = x + mixed @ w_mix_out[layer]

        h = rmsnorm(x, g_ffn[layer])
        if layer % 2 == 0:
            i = layer // 2
            f = swiglu(h, ffn_w1[i], ffn_w3[i], ffn_w2[i])
        else:
            i = layer // 2
            f = moe_swiglu(h, moe_router[i], moe_w1[i], moe_w3[i], moe_w2[i])
        x = x + f
    return rmsnorm(x, g_final)


_drawn_inputs = setup_inputs


def setup_inputs(seed=0):
    import zlib

    import numpy as np

    out = dict(_drawn_inputs(seed))
    spreads = {}
    factors = {}
    for name, (base, spread) in spreads.items():
        noise = np.random.default_rng([zlib.crc32(name.encode()), seed]).standard_normal(out[name].shape)
        drawn = base * np.exp(spread * noise) if base else spread * noise
        out[name] = __import__('jax').numpy.asarray(drawn.astype(out[name].dtype))
    for name, factor in factors.items():
        out[name] = (out[name] * factor).astype(out[name].dtype)
    return out
```

```python
from contextlib import ExitStack

import numpy as np

import concourse.bass as bass
from concourse import mybir

F32 = mybir.dt.float32
F32R = mybir.dt.float32r
I32 = mybir.dt.int32
U8 = mybir.dt.uint8
ALU = mybir.AluOpType
ACT = mybir.ActivationFunctionType
AX = mybir.AxisListType.X
ds = bass.ds

P = 128
D = 1024
SEQ = 256
NT = SEQ // P
KD = D // P
EPS = 1e-6
DEPTH = 2
HD = 64
NH = 4
DV = 128
RANK = 16
CONV = 256
EXPERTS = 8
F_DENSE = 2816
F_EXPERT = 3584
FC = 512
BLOCK = 2048
LEVELS = 7
CAP = P
FAR = -1.0e30
DILATED_PATTERNS = ((128, 1), (512, 4), (2048, 16))
REL_BUCKETS = 32
REL_MAX_DISTANCE = 2048

C_AQ, C_AK, C_AV = 0, 256, 512
C_GQ, C_GK, C_GV, C_GR = 768, 1024, 1280, 1792
C_LR, C_IN, C_B, C_C = 2304, 2320, 2576, 2832

MIX_IN = [(C_AQ, 512, 0, 4), (C_AQ, 512, 4, 4),
          (C_LR, 272, 0, 4), (C_LR, 272, 4, 4),
          (C_GQ, 512, 0, 4), (C_GQ, 512, 4, 4),
          (C_AV, 256, 0, 8),
          (C_GV, 512, 0, 4), (C_GV, 512, 4, 4),
          (C_GR, 512, 0, 4), (C_GR, 512, 4, 4),
          (C_B, 512, 0, 4), (C_B, 512, 4, 4)]
OUT_ROWS = [0, 768, 256, 512]
N_IN = len(MIX_IN)
N_MIX = N_IN + len(OUT_ROWS)
DENSE_FULL = F_DENSE // FC
HALF = F_DENSE - DENSE_FULL * FC
N_DENSE_BLOCKS = 6 * DENSE_FULL + 3
BASE = [0, N_MIX + N_DENSE_BLOCKS]
DENSE0 = N_MIX
MOE0 = BASE[1] + N_MIX
CHUNKS = F_EXPERT // FC
PER_EXPERT = 6 * CHUNKS
SLOTS = 6
RAW_FIXED = 3

K_ID, K_LEV, K_IOTA, K_DOWN = 0, P, P + 9 * P, P + 10 * P
K_COLS = K_DOWN + 16


def block_size(n):
    m = n - BASE[1] if n >= BASE[1] else n
    if m < N_IN:
        return MIX_IN[m][1] * MIX_IN[m][3]
    return BLOCK


def raw_plan():
    slot, use, before, count, last = {}, {}, {}, [0] * SLOTS, [None] * SLOTS
    for n in range(MOE0 + 2 * PER_EXPERT):
        m = n - BASE[1] if n >= BASE[1] else n
        s = (m + 1) % RAW_FIXED if m < N_MIX else (m - N_MIX) % SLOTS
        slot[n], before[n] = s, last[s]
        count[s] += 1
        use[n], last[s] = count[s], n
    return slot, use, before


def shape_constants():
    c = np.zeros((P, K_COLS), np.float32)
    c[:, K_ID:K_ID + P] = np.eye(P)
    s, t = np.meshgrid(np.arange(P), np.arange(P), indexing="ij")
    masks = np.zeros((P, LEVELS * P), np.int32)
    for level in range(LEVELS):
        half = 1 << level
        mid = t // (2 * half) * (2 * half) + half
        between = np.where(t >= mid, (s >= mid) & (s <= t), (s > t) & (s < mid))
        c[:, K_LEV + level * P:K_LEV + (level + 1) * P] = between
        masks[:, level * P:(level + 1) * P] = (s // (2 * half) == t // (2 * half)) & (s < mid) & (t >= mid)
    c[:, K_LEV + 7 * P:K_LEV + 8 * P] = s > t
    c[:, K_LEV + 8 * P:K_LEV + 9 * P] = s <= t
    c[:, K_IOTA:K_IOTA + P] = np.arange(P)
    c[:, K_DOWN:K_DOWN + 16] = np.tile(np.arange(EXPERTS, 0, -1), 2)
    onehot = np.zeros((REL_BUCKETS + 1, 512), np.float32)
    dist = 255 - np.arange(512)
    exact = REL_BUCKETS // 2
    d = np.maximum(dist, 0)
    ratio = np.log(np.maximum(d, 1).astype(np.float32) / exact) / np.float32(np.log(REL_MAX_DISTANCE / exact))
    large = np.minimum(exact + (ratio * (REL_BUCKETS - exact)).astype(np.int32), REL_BUCKETS - 1)
    onehot[np.where(d < exact, d, large), np.arange(512)] = 1.0
    held = sum(((dist >= 0) & (dist % dil == 0) & (dist // dil <= win // dil)).astype(np.int32)
               for win, dil in DILATED_PATTERNS)
    onehot[REL_BUCKETS] = np.where(held > 0, np.log(np.maximum(held, 1)), FAR)
    return c, masks, onehot


def trunk(nc, x_in, w_mix_in, w_mix_out, g_mix, rel_bias, gla_w_gate, gla_b_gate, gla_g_norm, conv_w,
          g_ffn, ffn_w1, ffn_w3, ffn_w2, moe_router, moe_w1, moe_w3, moe_w2, g_final,
          consts_in, masks_in, onehot_in, out):
    raw_slot, raw_use, raw_before = raw_plan()
    ctx = ExitStack()
    with ctx:
        at = [(nc.sbuf_base + 31) // 32 * 32]

        def place(name, cols, dt=F32, offset=None):
            size = 1 if dt == U8 else 4
            where = at[0] if offset is None else offset
            t = nc.alloc_sbuf_tensor_at(name, [P, cols], dt, offset=where)
            if offset is None:
                at[0] += (cols * size + 31) // 32 * 32
            return t

        raw = [place(f"raw{i}", BLOCK) for i in range(RAW_FIXED)]
        whi = [place(f"whi{i}", BLOCK, F32R) for i in range(SLOTS)]
        wlo = [place(f"wlo{i}", BLOCK, F32R) for i in range(SLOTS)]
        x = place("x", NT * D)
        h_at = at[0]
        h = place("h", NT * D)
        f_at = at[0]
        f_hi = place("f_hi", KD * SEQ, F32R)
        f_lo = place("f_lo", KD * SEQ, F32R)
        consts = place("consts", K_COLS)
        masks = place("masks", LEVELS * P, U8)
        small = place("small", 224)
        router_hi = place("router_hi", 64, F32R)
        router_lo = place("router_lo", 64, F32R)
        arena = at[0]

        gv = place("gv", NT * NH * DV, offset=h_at)
        gr = place("gr", NT * NH * DV, offset=h_at + 4096)
        g_row = place("g_row", D)
        ffn_arena = at[0]
        qT = place("qT", 512)
        kT = place("kT", 512)
        pt_tail = place("pt_tail", 512)
        av = place("av", 512)
        bias0 = place("bias0", NH * P)
        bias1 = place("bias1", NH * 2 * P)
        qk_tail = place("qk_tail", 512)
        prob0 = place("prob0", NH * P)
        prob1 = place("prob1", NH * 2 * P)
        gqT = place("gqT", 512)
        gkT = place("gkT", 512)
        log_a = place("log_a", 512)
        decay = place("decay", 512)
        scores = place("scores", 1024)
        cross = place("cross", 512)
        cin = place("cin", 512)
        cy = place("cy", 512)
        glr = place("glr", 256)
        w_gate = place("w_gate", 512)
        mix_end = at[0]
        base = {t: o for t, o in (("qT", ffn_arena), ("bias0", ffn_arena + 4 * 2048))}
        pT = place("pT", 1536, offset=base["qT"])
        qk_level = place("qk_level", 2048, offset=base["bias0"])
        go = place("go", 1024, offset=base["bias0"] + 4 * 2048)
        z_a = place("z_a", 512, offset=base["bias0"] + 4 * 2048 + 3 * 2048 + 4 * 2048)
        z_b = place("z_b", 512, offset=base["bias0"] + 4 * 2048 + 3 * 2048 + 5 * 2048)
        setup_hot = place("setup_hot", 512, offset=base["bias0"] + 4 * 2048)
        setup_rel = place("setup_rel", 8, offset=base["bias0"] + 5 * 2048)
        setup_wide = place("setup_wide", NH * P, offset=base["bias0"] + 6 * 2048)
        setup_bias = place("setup_bias", NH * 512, offset=base["qT"])
        setup_masks = place("setup_masks", LEVELS * P, I32, offset=base["bias0"] + 4 * 2048 + 3 * 2048 + 4 * 2048)
        setup_router = place("setup_router", 64, offset=base["bias0"] + 5 * 2048 + 256)

        at[0] = ffn_arena
        raw += [place(f"raw{i}", BLOCK) for i in range(RAW_FIXED, SLOTS)]
        gate_out = [place(f"gate_out{i}", FC) for i in range(2)]
        gT_at = at[0]
        gT_hi = [place(f"gT_hi{i}", FC, F32R) for i in range(2)]
        gT_lo = [place(f"gT_lo{i}", FC, F32R) for i in range(2)]
        dense_end = at[0]
        at[0] = gT_at + 2 * 4 * FC
        e_gT_hi = gT_hi[0]
        e_gT_lo = place("e_gT_lo", FC, F32R, offset=gT_at + 4 * FC)
        xe_hi = place("xe_hi", KD * P, F32R)
        xe_lo = place("xe_lo", KD * P, F32R)
        pick = place("pick", NT * P, F32R)
        pickT = place("pickT", NT * P, F32R)
        moe_end = at[0]
        assert max(mix_end, dense_end, moe_end) <= nc.sbuf_usable_end, (mix_end, dense_end, moe_end)
        xn_hi = place("xn_hi", NT * D, F32R, offset=f_at)
        xn_lo = place("xn_lo", NT * D, F32R, offset=f_at + 4 * NT * D)
        y_hi = place("y_hi", D, F32R, offset=h_at)
        y_lo = place("y_lo", D, F32R, offset=h_at + 4 * D)

        sq, ms, rs = small[:, 0:2], small[:, 2:4], small[:, 4:6]
        sq8, ms8, rs8 = small[:, 8:16], small[:, 16:24], small[:, 24:32]
        top, neg, rsum, rinv = small[:, 32:40], small[:, 40:48], small[:, 48:56], small[:, 56:64]
        power = small[:, 64:72]
        conv_k = small[:, 72:84]
        gnorm = small[:, 84:86]
        logit = small[:, 88:104]
        hot1, hot2, key, second = small[:, 104:120], small[:, 120:136], small[:, 136:152], small[:, 152:168]
        m1, m2, r1, r2 = small[:, 168:170], small[:, 170:172], small[:, 172:174], small[:, 174:176]
        gdiff, gexp, g1, g2 = small[:, 176:178], small[:, 178:180], small[:, 180:182], small[:, 182:184]
        chosen = small[:, 184:200]
        small2 = nc.alloc_sbuf_tensor_at("small2", [P, 64], F32, offset=max(mix_end, dense_end, moe_end))
        assert max(mix_end, dense_end, moe_end) + 64 * 4 + 512 + 64 <= nc.sbuf_usable_end
        gates, place1, place2, most = small2[:, 0:16], small2[:, 16:32], small2[:, 32:48], small2[:, 48:49]
        most_int = nc.alloc_sbuf_tensor_at("most_int", [P, 8], I32, offset=max(mix_end, dense_end, moe_end) + 256)
        ones = nc.alloc_sbuf_tensor_at("ones", [P, P], F32, offset=max(mix_end, dense_end, moe_end) + 288)

        bank = [ctx.enter_context(nc.psum_tensor(f"bank{i}", [P, 512], F32)) for i in range(8)]
        bias_dram = nc.dram_tensor("bias_by_distance", [P, NH * 512], F32).ap()

        def sem(name):
            return ctx.enter_context(nc.semaphore(name))

        raw_full = [sem(f"raw_full{i}") for i in range(SLOTS)]
        hi_ready, lo_ready, block_used = sem("hi_ready"), sem("lo_ready"), sem("block_used")
        x_loaded, consts_loaded, params_loaded = sem("x_loaded"), sem("consts_loaded"), sem("params_loaded")
        hot_loaded, gains_loaded = sem("hot_loaded"), sem("gains_loaded")
        gate_loaded = sem("gate_loaded")
        bias_ps, bias_sb, bias_stored, bias_loaded = (sem(n) for n in ("bias_ps", "bias_sb", "bias_stored", "bias_loaded"))
        ones_set, power_set, router_split = sem("ones_set"), sem("power_set"), sem("router_split")
        masks_set = sem("masks_set")
        x_ready, squares, means, roots, h_ready = (sem(n) for n in ("x_ready", "squares", "means", "roots", "h_ready"))
        hT_ps, hT_hi, hT_ready = sem("hT_ps"), sem("hT_hi"), sem("hT_ready")
        q_ps, glr_ps, gq_ps, z_ps = (sem(n) for n in ("q_ps", "glr_ps", "gq_ps", "z_ps"))
        qk_sb, glr_sb, cin_sb, gqk_sb, av_sb, ln_sb = (sem(n) for n in ("qk_sb", "glr_sb", "cin_sb", "gqk_sb", "av_sb", "ln_sb"))
        log_ready, e_ps, decay_sb, level_sb, s_ps, s_sb = (sem(n) for n in ("log_ready", "e_ps", "decay_sb", "level_sb", "s_ps", "s_sb"))
        att_ps, logits_sb, top_sb, exp_sb, prob_ready = (sem(n) for n in ("att_ps", "logits_sb", "top_sb", "exp_sb", "prob_ready"))
        pT_ps, pT_sb, atto_ps = sem("pT_ps"), sem("pT_sb"), sem("atto_ps")
        gv_ps, gv_sb, gr_ps, gr_sb, gr_silu = (sem(n) for n in ("gv_ps", "gv_sb", "gr_ps", "gr_sb", "gr_silu"))
        conv_sb, o_ps, sq8_sb, ms8_sb, rs8_sb, go_sb, go_ps = (
            sem(n) for n in ("conv_sb", "o_ps", "sq8_sb", "ms8_sb", "rs8_sb", "go_sb", "go_ps"))
        mix_hi, mix_ready = sem("mix_hi"), sem("mix_ready")
        h1_ps, h3_ps, silu_sb, g_ready, gT_ps, gT_h, gT_ready, y_ps = (
            sem(n) for n in ("h1_ps", "h3_ps", "silu_sb", "g_ready", "gT_ps", "gT_h", "gT_ready", "y_ps"))
        logit_ps, gdiff_sb, gexp_sb, chosen_sb, place_ps, place_sb, count_sb, xn_h, xn_ready = (
            sem(n) for n in ("logit_ps", "gdiff_sb", "gexp_sb", "chosen_sb", "place_ps", "place_sb", "count_sb", "xn_h", "xn_ready"))
        e_silu, e_g, e_gT_ps, e_gT_h, e_gT = (
            sem(n) for n in ("e_silu", "e_g", "e_gT_ps", "e_gT_h", "e_gT"))
        pick_sb, xe_ps, xe_h, xe_ready, pickT_ps, pickT_sb = (
            sem(n) for n in ("pick_sb", "xe_ps", "xe_h", "xe_ready", "pickT_ps", "pickT_sb"))
        y_h, y_ready, back_ps, added = (sem(n) for n in ("y_h", "y_ready", "back_ps", "added"))
        rel_set = sem("rel_set")
        act_step, dve_step = sem("act_step"), sem("dve_step")
        stored = sem("stored")

        def ident():
            return consts[:, K_ID:K_ID + P]

        def lev(i):
            return consts[:, K_LEV + i * P:K_LEV + (i + 1) * P]

        block = ctx.enter_context(nc.Block())

        def expert_block(t, k):
            return t * PER_EXPERT + (MOE0 + k)

        def hidden(engine, c, t, i, turn):
            if t == 0:
                engine.wait_ge((h1_ps, h3_ps)[i], turn + (c + 1))
            else:
                per = 2 if c < DENSE_FULL else 1
                engine.wait_ge(block_used, 6 * turn + (DENSE0 + 6 * c + per * (i + 1)))

        @block.sync
        def _(sp):
            def fill(n, src, rows, cols, turn=0, per=0, uses=0):
                s = raw_slot[n]
                before = n - SLOTS if n >= MOE0 + 4 or per == PER_EXPERT else raw_before[n]
                dst = raw[s][:, 0:rows * cols].rearrange("p (k c) -> p k c", k=rows)
                until = None if before is None else sp.lower_val(per * turn + before + 1)
                load = sp.dma_start(dst, src)
                if until is not None:
                    load.wait_op(lo_ready, until, "sem-ge")
                load.then_inc(raw_full[s], 16)

            def ktiles(w):
                return w.rearrange("(k p) c -> p k c", p=P)

            def mixer(l):
                b = BASE[l]
                w = ktiles(w_mix_in[l])
                for i, (c, nc_, k, nk) in enumerate(MIX_IN):
                    fill(b + i, w[:, k:k + nk, c:c + nc_], nk, nc_)
                wo = w_mix_out[l]
                for i, r in enumerate(OUT_ROWS):
                    fill(b + N_IN + i, ktiles(wo[r:r + 2 * P, :]), 2, D)

            def dense_chunk(c, turn):
                n = DENSE0 + 6 * c
                cols = ds(turn * FC + c * FC, FC)
                for i, w in enumerate((ffn_w1, ffn_w3)):
                    for k in range(2):
                        if c == 0 and i == 1 and k == 1:
                            sp.wait_ge(mix_ready, 4)
                        fill(n + 2 * i + k, ktiles(w[0])[:, 4 * k:4 * k + 4, cols], 4, FC, turn, 6)
                for k in range(2):
                    rows = ffn_w2[0][ds(turn * FC + (c * FC + 2 * P * k), 2 * P), :]
                    fill(n + 4 + k, ktiles(rows), 2, D, turn, 6)

            def expert(sweep, e, last=False, turn=0):
                n = MOE0
                t = EXPERTS * sweep + turn + e
                for c in range(CHUNKS):
                    if c:
                        first_two(n + 6 * c - 2, e, turn, t, c, 0)
                    if c:
                        for k in range(2):
                            fill_w2(n + 6 * c + 2 + k, e, turn, t, c - 1, k)
                for k in range(2):
                    fill_w2(n + 40 + k, e, turn, t, CHUNKS - 1, k)
                if not last:
                    first_two(n + PER_EXPERT, e + 1, turn, t, 0, 0)

            def first_two(n, e, turn, t, c, _):
                for i, w in enumerate((moe_w1, moe_w3)):
                    for k in range(2):
                        src = w[0].rearrange("e (k p) c -> p e k c", p=P)
                        src = src[:, ds(turn + e, 1), 4 * k:4 * k + 4, c * FC:(c + 1) * FC]
                        fill(n + 2 * i + k, src.rearrange("p e k c -> p (e k) c"), 4, FC, t, PER_EXPERT)

            def fill_w2(n, e, turn, t, c, k):
                src = moe_w2[0].rearrange("e (k p) c -> p e k c", p=P)
                src = src[:, ds(turn + e, 1), 4 * c + 2 * k:4 * c + 2 * k + 2, :]
                fill(n, src.rearrange("p e k c -> p (e k) c"), 2, D, t, PER_EXPERT)

            def sweep_experts(sweep):
                if sweep:
                    first_two(MOE0, 0, 0, EXPERTS * sweep, 0, 0)
                with sp.Fori(0, EXPERTS - 1) as e:
                    expert(sweep, 0, turn=e)
                expert(sweep, EXPERTS - 1, last=True)

            mixer(0)
            dense_chunk(0, 0)
            dense_chunk(1, 0)
            with sp.Fori(0, DENSE_FULL - 3) as c:
                dense_chunk(2, c)
            dense_chunk(DENSE_FULL - 1, 0)
            n = DENSE0 + 6 * DENSE_FULL
            for i, w in enumerate((ffn_w1, ffn_w3)):
                fill(n + i, ktiles(w[0])[:, :, DENSE_FULL * FC:], KD, HALF)
            fill(n + 2, ktiles(ffn_w2[0][DENSE_FULL * FC:, :]), 2, D)
            mixer(1)
            for i, w in enumerate((moe_w1, moe_w3)):
                for k in range(2):
                    if i == 1 and k == 1:
                        sp.wait_ge(mix_ready, 8)
                    src = w[0][0].rearrange("(k p) c -> p k c", p=P)[:, 4 * k:4 * k + 4, 0:FC]
                    fill(MOE0 + 2 * i + k, src, 4, FC)
            sweep_experts(0)
            sp.wait_ge(count_sb, 1)
            count = sp.value_load(most_int[0:1, 0:1], min_val=0, max_val=SEQ)
            with sp.If(count > CAP):
                sweep_experts(1)
            sp.wait_ge(h_ready, 10)
            sp.dma_start(out.rearrange("b (t p) d -> p (b t) d", p=P),
                         h[:].rearrange("p (t d) -> p t d", t=NT)).then_inc(stored, 16)
            sp.wait_ge(stored, 16)

        @block.gpsimd
        def _(pool):
            pool.dma_start(x[:].rearrange("p (t d) -> p t d", t=NT),
                           x_in.rearrange("b (t p) d -> p (b t) d", p=P)).then_inc(x_loaded, 16)

            def gains(row):
                pool.dma_start(g_row[:], bass.AP(tensor=row.tensor, offset=row.offset, ap=[[0, P], [1, D]])
                               ).then_inc(gains_loaded, 16)

            def gate_weights(l):
                g = w_gate[:, 0:256]
                pool.dma_start(g[0:RANK, :], gla_w_gate[l]).then_inc(gate_loaded, 16)
                pool.dma_start(g[RANK:RANK + 1, :], gla_b_gate[l:l + 1, :]).then_inc(gate_loaded, 16)

            def bias_tiles(l):
                for i, (tile_, n) in enumerate(((bias0, P), (bias1, 2 * P))):
                    src = bass.AP(tensor=bias_dram.tensor, offset=255 - P * i, ap=[[NH * 512 - 1, P], [512, NH], [1, n]])
                    pool.dma_start(tile_[:].rearrange("p (h s) -> p h s", h=NH), src).then_inc(bias_loaded, 16)

            gains(g_mix[0])
            pool.dma_start(consts[:], consts_in).then_inc(consts_loaded, 16)
            pool.dma_start(setup_hot[0:REL_BUCKETS + 1, :], onehot_in).then_inc(hot_loaded, 16)
            pool.dma_start(setup_rel[0:REL_BUCKETS, 0:NH], rel_bias).then_inc(hot_loaded, 16)
            pool.dma_start(setup_masks[:], masks_in).then_inc(params_loaded, 16)
            pool.dma_start(conv_k, conv_w).then_inc(params_loaded, 16)
            pool.dma_start(gnorm, gla_g_norm).then_inc(params_loaded, 16)
            pool.dma_start(setup_router[:].rearrange("p (k e) -> p k e", k=KD),
                           moe_router[0].rearrange("(k p) e -> p k e", p=P)).then_inc(params_loaded, 16)
            nc.gpsimd.memset(power, -0.5).then_inc(power_set, 1)
            pool.wait_ge(ones_set, 3)
            gate_weights(0)
            pool.wait_ge(bias_sb, NH)
            pool.dma_start(bias_dram, setup_bias[:]).then_inc(bias_stored, 16)
            pool.wait_ge(bias_stored, 16)
            bias_tiles(0)

            def root(i):
                pool.wait_ge(means, i + 1)
                nc.gpsimd.tensor_tensor(rs, ms, power[:, 0:2], ALU.pow).then_inc(roots, 1)

            def head_roots(l):
                pool.wait_ge(ms8_sb, l + 1)
                nc.gpsimd.tensor_tensor(rs8, ms8, power, ALU.pow).then_inc(rs8_sb, 1)

            pool.wait_ge(power_set, 1)
            root(0)
            pool.wait_ge(h_ready, 2)
            gains(g_ffn[0])
            head_roots(0)
            root(1)
            pool.wait_ge(h_ready, 4)
            gains(g_mix[1])
            pool.wait_ge(x_ready, 2)
            pool.wait_ge(ones_set, 4)
            gate_weights(1)
            bias_tiles(1)
            root(2)
            pool.wait_ge(h_ready, 6)
            gains(g_ffn[1])
            head_roots(1)
            root(3)
            pool.wait_ge(h_ready, 8)
            gains(g_final)
            root(4)

        @block.scalar
        def _(act):
            def split(n, turn=0, per=0):
                s, w = raw_slot[n], n % SLOTS
                size = block_size(n)
                act.wait_ge(raw_full[s], 16 * (per // SLOTS) * turn + 16 * raw_use[n])
                if n >= SLOTS:
                    act.wait_ge(block_used, per * turn + n - SLOTS + 1)
                nc.scalar.copy(whi[w][:, 0:size], raw[s][:, 0:size]).then_inc(hi_ready, 1)

            def norm_squares(i):
                act.wait_ge(x_ready, i) if i else act.wait_ge(x_loaded, 16)
                if i:
                    act.wait_ge(h_ready, 2 * i)
                for t in range(NT):
                    nc.scalar.activation(h[:, t * D:(t + 1) * D], x[:, t * D:(t + 1) * D], ACT.Square,
                                         accum_out=sq[:, t:t + 1]).then_inc(squares, 1)

            def turn_hi(i):
                for j in range(4):
                    act.wait_ge(hT_ps, 4 * i + j + 1)
                    nc.scalar.copy(f_hi[:, 512 * j:512 * (j + 1)], bank[j][:]).then_inc(hT_hi, 1)

            step = [0]

            def link(ins):
                step[0] += 1
                ins.then_inc(act_step, 1)
                act.wait_ge(act_step, step[0])

            def mixer(l):
                b = BASE[l]
                norm_squares(2 * l)
                turn_hi(2 * l)
                act.wait_ge(q_ps, l + 1)
                act.wait_ge(bias_stored, 16)
                nc.scalar.copy(qT[:], bank[0][:]).then_inc(qk_sb, 1)
                act.wait_ge(block_used, b + 2)
                nc.scalar.copy(kT[:], bank[1][:]).then_inc(qk_sb, 1)
                split(b + 6)
                split(b + 7)
                act.wait_ge(glr_ps, l + 1)
                act.wait_ge(ones_set, 3 + l)
                nc.scalar.copy(glr[0:RANK, :], bank[2][0:RANK, 0:256]).then_inc(glr_sb, 1)
                act.wait_ge(block_used, b + 4)
                nc.scalar.copy(cin[:], bank[3][:]).then_inc(cin_sb, 1)
                split(b + 8)
                split(b + 9)
                act.wait_ge(gq_ps, l + 1)
                nc.scalar.mul(gqT[:], bank[4][:], HD ** -0.5).then_inc(gqk_sb, 1)
                act.wait_ge(block_used, b + 6)
                nc.scalar.copy(gkT[:], bank[5][:]).then_inc(gqk_sb, 1)
                split(b + 10)
                split(b + 11)
                act.wait_ge(z_ps, l + 1)
                link(nc.scalar.activation(z_a[:], bank[7][:], ACT.Abs))
                link(nc.scalar.activation(z_b[:], z_a[:], ACT.Exp, scale=-1.0))
                nc.scalar.activation(z_a[:], z_b[:], ACT.Ln, bias=1.0).then_inc(ln_sb, 1)
                act.wait_ge(block_used, b + 7)
                nc.scalar.copy(av[:], bank[6][:]).then_inc(av_sb, 1)
                split(b + 12)
                for t in range(NT):
                    act.wait_ge(top_sb, 2 * l + t + 1)
                    src, n = ((prob0, P), (prob1, 2 * P))[t]
                    for hh in range(NH):
                        c = NH * t + hh
                        ins = nc.scalar.activation(src[:, hh * n:(hh + 1) * n], src[:, hh * n:(hh + 1) * n], ACT.Exp,
                                                   bias=neg[:, c:c + 1], accum_out=rsum[:, c:c + 1])
                    ins.then_inc(exp_sb, 1)

                def level_decay(i):
                    act.wait_ge(e_ps, 8 * l + i + 1)
                    act.wait_ge(level_sb, 8 * l + i) if 8 * l + i else None
                    nc.scalar.activation(decay[:], bank[(4, 7)[i % 2]][:], ACT.Exp).then_inc(decay_sb, 1)

                level_decay(0)
                split(b + 13)
                split(b + 14)
                for t in range(NT):
                    act.wait_ge(gv_ps, l + 1) if t == 0 else act.wait_ge(block_used, b + 9)
                    nc.scalar.copy(gv[:, 512 * t:512 * (t + 1)], bank[5 + t][:]).then_inc(gv_sb, 1)
                for j in range(3):
                    act.wait_ge(pT_ps, 3 * l + j + 1)
                    nc.scalar.copy(pT[:, 512 * j:512 * (j + 1)], bank[j][:]).then_inc(pT_sb, 1)
                level_decay(1)
                for t in range(NT):
                    act.wait_ge(gr_ps, l + 1) if t == 0 else act.wait_ge(block_used, b + 11)
                    nc.scalar.copy(gr[:, 512 * t:512 * (t + 1)], bank[(3, 5)[t]][:]).then_inc(gr_sb, 1)
                split(b + 15)
                split(b + 16)
                for i in range(2, LEVELS + 1):
                    level_decay(i)
                    if i == 4:
                        act.wait_ge(block_used, b + 13)
                        act.wait_ge(atto_ps, l + 1)
                        nc.scalar.copy(f_hi[:, 0:512], bank[0][:]).then_inc(mix_hi, 1)
                split(b + 17)
                split(b + 18)
                act.wait_ge(conv_sb, l + 1)
                nc.scalar.copy(f_hi[:, 512:1024], cy[:]).then_inc(mix_hi, 1)
                act.wait_ge(gr_sb, 2 * l + 2)
                nc.scalar.activation(gr[:], gr[:], ACT.Silu).then_inc(gr_silu, 1)
                for t in range(NT):
                    act.wait_ge(o_ps, 2 * l + t + 1)
                    for hh in range(NH):
                        c = NH * t + hh
                        ins = nc.scalar.activation((decay, log_a)[t][:, hh * P:(hh + 1) * P], bank[3 + t][:, hh * P:(hh + 1) * P], ACT.Square,
                                                   accum_out=sq8[:, c:c + 1])
                ins.then_inc(sq8_sb, 1)
                for j in range(2):
                    act.wait_ge(go_ps, 2 * l + j + 1)
                    nc.scalar.activation(f_hi[:, 1024 + 512 * j:1536 + 512 * j], bank[5 + j][:], ACT.Copy,
                                         scale=gnorm[:, l:l + 1]).then_inc(mix_hi, 1)
                split(b + 19)
                split(b + 20)

            def d_silu(c, t, turn=0, width=FC):
                hidden(act, c, t, 0, turn)
                nc.scalar.activation(gate_out[t][:, 0:width], bank[2 * t][:, 0:width], ACT.Silu).then_inc(silu_sb, 1)

            def d_gT(c, t, turn=0, width=FC):
                act.wait_ge(gT_ps, 2 * turn + 2 * c + t + 1)
                nc.scalar.copy(gT_hi[t][:, 0:width], bank[2 * t][:, 0:width]).then_inc(gT_h, 1)

            def dense_chunk(c, turn=0):
                n = DENSE0 + 6 * c
                width = FC if c < DENSE_FULL else HALF
                if c:
                    d_silu(c - 1, 1, turn)
                    d_gT(c - 1, 1, turn)
                d_silu(c, 0, turn, width)
                if c < DENSE_FULL:
                    for k in range(2):
                        split(n + 4 + k, turn, 6)
                    d_gT(c, 0, turn)
                    for k in range(4 if c < DENSE_FULL - 1 else 2):
                        split(n + 6 + k, turn, 6)
                else:
                    split(n + 2)
                    d_gT(c, 0, 0, width)
                    for k in range(3):
                        split(BASE[1] + k)
                    d_silu(c, 1, 0, width)
                    d_gT(c, 1, 0, width)
                    for k in range(3, 6):
                        split(BASE[1] + k)

            def e_silu_(c, t):
                act.wait_ge(block_used, expert_block(t, 6 * c if c else 2))
                nc.scalar.activation(gate_out[c % 2][:], bank[2 * (c % 2)][:], ACT.Silu).then_inc(e_silu, 1)

            def e_gT_hi_(c, u):
                act.wait_ge(e_gT_ps, u + c + 1)
                nc.scalar.copy(e_gT_hi[:], bank[2 * (c % 2)][:]).then_inc(e_gT_h, 1)

            def gathered(v):
                for j in range(2):
                    act.wait_ge(xe_ps, v + j + 1)
                    nc.scalar.copy(xe_hi[:, 512 * j:512 * (j + 1)], bank[6 + j][:]).then_inc(xe_h, 1)

            def pick_turned(v):
                act.wait_ge(pickT_ps, v + 1)
                nc.scalar.copy(pickT[:], bank[2][:, 0:NT * P]).then_inc(pickT_sb, 1)

            def expert(sweep, e, turn=0, last=False):
                t = turn + (EXPERTS * sweep + e)
                u = t * CHUNKS

                def sp_(k):
                    split(MOE0 + k, t, PER_EXPERT)

                for k in range(4, 8):
                    sp_(k)
                for c in range(1, CHUNKS):
                    e_silu_(c - 1, t)
                    sp_(6 * c + 2)
                    sp_(6 * c + 3)
                    e_gT_hi_(c - 1, u)
                    if c < CHUNKS - 1:
                        for k in range(4):
                            sp_(6 * c + 4 + k)
                    else:
                        for k in range(2 if last else 4):
                            sp_(40 + k)
                e_silu_(CHUNKS - 1, t)
                if not last:
                    gathered(t * 2 + 2)
                e_gT_hi_(CHUNKS - 1, u)
                if not last:
                    sp_(44)
                    sp_(45)
                for j in range(2):
                    act.wait_ge(block_used, expert_block(t, PER_EXPERT))
                    nc.scalar.copy(y_hi[:, 512 * j:512 * (j + 1)], bank[4 + j][:]).then_inc(y_h, 1)
                if not last:
                    pick_turned(t + 1)

            def sweep_experts(sweep):
                if sweep:
                    for k in range(4):
                        split(MOE0 + k, EXPERTS * sweep, PER_EXPERT)
                gathered(2 * EXPERTS * sweep)
                pick_turned(EXPERTS * sweep)
                with act.Fori(0, EXPERTS - 1) as e:
                    expert(sweep, 0, turn=e)
                expert(sweep, EXPERTS - 1, last=True)

            for k in range(3):
                split(k)
            act.wait_ge(params_loaded, 64)
            nc.scalar.copy(router_hi[:], setup_router[:]).then_inc(router_split, 1)
            for k in range(3, 6):
                split(k)
            mixer(0)
            norm_squares(1)
            turn_hi(1)
            dense_chunk(0)
            dense_chunk(1)
            with act.Fori(0, DENSE_FULL - 3) as c:
                dense_chunk(2, c)
            dense_chunk(DENSE_FULL - 1)
            dense_chunk(DENSE_FULL)
            mixer(1)
            norm_squares(3)
            turn_hi(3)
            act.wait_ge(logit_ps, 1)
            for t in range(NT):
                nc.scalar.copy(xn_hi[:, t * D:(t + 1) * D], h[:, t * D:(t + 1) * D]).then_inc(xn_h, 1)
            act.wait_ge(gdiff_sb, 1)
            nc.scalar.activation(gexp, gdiff, ACT.Exp).then_inc(gexp_sb, 1)
            sweep_experts(0)
            act.wait_ge(count_sb, 1)
            count = act.value_load(most_int[0:1, 0:1], min_val=0, max_val=SEQ)
            with act.If(count > CAP):
                sweep_experts(1)
            norm_squares(4)

        @block.vector
        def _(dve):
            step = [0]

            def link(ins):
                step[0] += 1
                ins.then_inc(dve_step, 1)
                dve.wait_ge(dve_step, step[0])

            def split(n, turn=0, per=0):
                s, w = raw_slot[n], n % SLOTS
                size = block_size(n)
                dve.wait_ge(hi_ready, per * turn + n + 1)
                nc.vector.tensor_tensor(wlo[w][:, 0:size], raw[s][:, 0:size], whi[w][:, 0:size].bitcast(F32),
                                        ALU.subtract).then_inc(lo_ready, 1)

            def rest(dst, src, hi, sem_in, value, sem_out):
                dve.wait_ge(sem_in, value)
                nc.vector.tensor_tensor(dst, src, hi.bitcast(F32), ALU.subtract).then_inc(sem_out, 1)

            def norm_rows(i):
                dve.wait_ge(squares, 2 * i + 2)
                nc.vector.tensor_scalar(ms, sq, 1.0 / D, EPS, ALU.mult, ALU.add).then_inc(means, 1)
                dve.wait_ge(roots, i + 1)
                dve.wait_ge(gains_loaded, 16 * (i + 1))
                for t in range(NT):
                    nc.vector.scalar_tensor_tensor(h[:, t * D:(t + 1) * D], x[:, t * D:(t + 1) * D], rs[:, t:t + 1],
                                                   g_row[:], ALU.mult, ALU.mult).then_inc(h_ready, 1)

            def turn_lo(i):
                for j in range(4):
                    rest(f_lo[:, 512 * j:512 * (j + 1)], bank[j][:], f_hi[:, 512 * j:512 * (j + 1)],
                         hT_hi, 4 * i + j + 1, hT_ready)

            def ones_row(l):
                nc.vector.memset(glr[0:32, :], 1.0).then_inc(ones_set, 1)

            def mixer(l):
                b = BASE[l]
                norm_rows(2 * l)
                turn_lo(2 * l)
                split(b + 6)
                split(b + 7)
                split(b + 8)
                split(b + 9)
                split(b + 10)
                split(b + 11)
                dve.wait_ge(ln_sb, l + 1)
                link(nc.vector.scalar_tensor_tensor(log_a[:], bank[7][:], 0.0, z_a[:], ALU.min, ALU.subtract))
                nc.vector.tensor_scalar(log_a[:], log_a[:], 1.0 / 16.0, None, ALU.mult).then_inc(log_ready, 1)
                split(b + 12)
                dve.wait_ge(bias_loaded, 32 * (l + 1))
                for t in range(NT):
                    n = P * (t + 1)
                    dst = (prob0, prob1)[t][:].rearrange("p (a o s) -> p a o s", a=2, o=2)
                    bias = (bias0, bias1)[t][:].rearrange("p (a o s) -> p a o s", a=2, o=2)
                    for odd in range(2):
                        dve.wait_ge(att_ps, 4 * l + 2 * t + odd + 1)
                        src = bank[((0, 3), (1, 2))[t][odd]][:, 0:2 * n].rearrange("p (a s) -> p a s", a=2)
                        ins = nc.vector.scalar_tensor_tensor(dst[:, :, odd, :], src, HD ** -0.5, bias[:, :, odd, :],
                                                             ALU.mult, ALU.add)
                        ins.then_inc(logits_sb, 1)
                    dve.wait_ge(logits_sb, 4 * l + 2 * t + 2)
                    link(nc.vector.tensor_reduce(top[:, NH * t:NH * (t + 1)],
                                                 (prob0, prob1)[t][:].rearrange("p (h s) -> p h s", h=NH), AX, ALU.max))
                    nc.vector.tensor_scalar(neg[:, NH * t:NH * (t + 1)], top[:, NH * t:NH * (t + 1)], -1.0, None,
                                            ALU.mult).then_inc(top_sb, 1)
                for t in range(NT):
                    n = P * (t + 1)
                    dve.wait_ge(exp_sb, 2 * l + t + 1)
                    link(nc.vector.reciprocal(rinv[:, NH * t:NH * (t + 1)], rsum[:, NH * t:NH * (t + 1)]))
                    src = (prob0, prob1)[t]
                    for hh in range(NH):
                        c = NH * t + hh
                        ins = nc.vector.tensor_scalar(src[:, hh * n:(hh + 1) * n], src[:, hh * n:(hh + 1) * n],
                                                      rinv[:, c:c + 1], None, ALU.mult)
                    ins.then_inc(prob_ready, 1)

                def level_operands(i):
                    dve.wait_ge(decay_sb, 8 * l + i + 1)
                    if i >= 2:
                        dve.wait_ge(s_ps, 2 * (9 * l + i))
                    off = 1024 * (i % 2)
                    nc.vector.tensor_tensor(qk_level[:, off:off + 512], gqT[:], decay[:], ALU.mult)
                    nc.vector.tensor_tensor(qk_level[:, off + 512:off + 1024], gkT[:], decay[:],
                                            ALU.mult).then_inc(level_sb, 1)

                def level_scores(i):
                    for odd in range(2):
                        v = 18 * l + 2 * (i + 1) + odd + 1
                        dve.wait_ge(s_ps, v)
                        if i == LEVELS:
                            nc.vector.tensor_copy(cross[:, 256 * odd:256 * (odd + 1)],
                                                  bank[5 + odd][:, 0:256]).then_inc(s_sb, 1)
                            continue
                        dst = scores[:, 512 * odd:512 * (odd + 1)].rearrange("p (g t) -> p g t", g=4)
                        src = bank[5 + odd][:].rearrange("p (g t) -> p g t", g=4)
                        if i < 0:
                            one = ident().rearrange("p (g t) -> p g t", g=1).broadcast_to([P, 4, P])
                            nc.vector.tensor_tensor(dst, src, one, ALU.mult).then_inc(s_sb, 1)
                        else:
                            dve.wait_ge(s_sb, v - 2)
                            m = masks[:, i * P:(i + 1) * P].rearrange("p (g t) -> p g t", g=1).broadcast_to([P, 4, P])
                            nc.vector.copy_predicated(dst, m, src).then_inc(s_sb, 1)

                dve.wait_ge(gqk_sb, 2 * l + 2)
                level_operands(0)
                split(b + 13)
                split(b + 14)
                level_operands(1)
                split(b + 15)
                split(b + 16)
                dve.wait_ge(masks_set, 1)
                level_scores(-1)
                for i in range(LEVELS + 1):
                    level_scores(i)
                    if i + 2 <= LEVELS:
                        level_operands(i + 2)
                    if i == 2:
                        dve.wait_ge(block_used, b + 13)
                        dve.wait_ge(cin_sb, l + 1)
                        link(nc.vector.tensor_tensor(cin[:], cin[:], bank[2][:], ALU.mult))
                        w = conv_k[:, 6 * l:6 * l + 6]
                        for half in range(2):
                            o = 256 * half
                            ins = nc.vector.tensor_scalar(cy[:, o:o + 256], cin[:, o:o + 256],
                                                          w[:, 3 * half + 2:3 * half + 3], None, ALU.mult)
                        link(ins)
                        for back in (1, 2):
                            for half in range(2):
                                o = 256 * half
                                ins = nc.vector.scalar_tensor_tensor(
                                    cy[:, o + back:o + 256], cin[:, o:o + 256 - back],
                                    w[:, 3 * half + 2 - back:3 * half + 3 - back], cy[:, o + back:o + 256],
                                    ALU.mult, ALU.add)
                            link(ins)
                        nc.vector.tensor_tensor(cy[:], cy[:], bank[1][:], ALU.mult).then_inc(conv_sb, 1)
                rest(f_lo[:, 0:512], bank[0][:], f_hi[:, 0:512], mix_hi, 4 * l + 1, mix_ready)
                split(b + 17)
                split(b + 18)
                dve.wait_ge(conv_sb, l + 1)
                rest(f_lo[:, 512:1024], cy[:], f_hi[:, 512:1024], mix_hi, 4 * l + 2, mix_ready)
                dve.wait_ge(sq8_sb, l + 1)
                nc.vector.tensor_scalar(ms8, sq8, 1.0 / DV, EPS, ALU.mult, ALU.add).then_inc(ms8_sb, 1)
                dve.wait_ge(rs8_sb, l + 1)
                dve.wait_ge(gr_silu, l + 1)
                for t in range(NT):
                    for hh in range(NH):
                        c = NH * t + hh
                        ins = nc.vector.scalar_tensor_tensor(
                            go[:, c * P:(c + 1) * P], bank[3 + t][:, hh * P:(hh + 1) * P], rs8[:, c:c + 1],
                            gr[:, c * P:(c + 1) * P], ALU.mult, ALU.mult)
                ins.then_inc(go_sb, 1)
                for j in range(2):
                    dve.wait_ge(mix_hi, 4 * l + 3 + j)
                    o = 1024 + 512 * j
                    nc.vector.scalar_tensor_tensor(f_lo[:, o:o + 512], bank[5 + j][:], gnorm[:, l:l + 1],
                                                   f_hi[:, o:o + 512].bitcast(F32), ALU.mult,
                                                   ALU.subtract).then_inc(mix_ready, 1)
                split(b + 19)
                split(b + 20)
                dve.wait_ge(block_used, b + N_MIX)
                for i, bk in enumerate((0, 1, 2, 7)):
                    o = 512 * i
                    ins = nc.vector.tensor_tensor(x[:, o:o + 512], x[:, o:o + 512], bank[bk][:], ALU.add)
                ins.then_inc(x_ready, 1)

            def d_mult(c, t, turn=0, width=FC):
                u = 2 * c + t
                dve.wait_ge(silu_sb, 2 * turn + u + 1)
                hidden(dve, c, t, 1, turn)
                nc.vector.tensor_tensor(gate_out[t][:, 0:width], gate_out[t][:, 0:width], bank[2 * t + 1][:, 0:width],
                                        ALU.mult).then_inc(g_ready, 1)

            def d_gT(c, t, turn=0, width=FC):
                u = 2 * c + t
                rest(gT_lo[t][:, 0:width], bank[2 * t][:, 0:width], gT_hi[t][:, 0:width],
                     gT_h, 2 * turn + u + 1, gT_ready)

            def dense_chunk(c, turn=0):
                n = DENSE0 + 6 * c
                width = FC if c < DENSE_FULL else HALF
                if c:
                    d_mult(c - 1, 1, turn)
                    d_gT(c - 1, 1, turn)
                d_mult(c, 0, turn, width)
                if c < DENSE_FULL:
                    for k in range(2):
                        split(n + 4 + k, turn, 6)
                    d_gT(c, 0, turn)
                    for k in range(4 if c < DENSE_FULL - 1 else 2):
                        split(n + 6 + k, turn, 6)
                else:
                    split(n + 2)
                    d_gT(c, 0, 0, width)
                    for k in range(3):
                        split(BASE[1] + k)
                    d_mult(c, 1, 0, width)
                    d_gT(c, 1, 0, width)
                    for k in range(3, 6):
                        split(BASE[1] + k)
                    for t in range(NT):
                        dve.wait_ge(y_ps, c + 1) if t == 0 else dve.wait_ge(block_used, BASE[1])
                        for j in range(2):
                            o = D * t + 512 * j
                            ins = nc.vector.tensor_tensor(x[:, o:o + 512], x[:, o:o + 512], bank[4 + 2 * t + j][:],
                                                          ALU.add)
                    ins.then_inc(x_ready, 1)

            def route():
                dve.wait_ge(logit_ps, 1)
                link(nc.vector.tensor_copy(logit, bank[4][:, 0:16]))
                down = consts[:, K_DOWN:K_DOWN + EXPERTS]
                for src, m, r, hot in ((logit, m1, r1, hot1), (second, m2, r2, hot2)):
                    if src is second:
                        link(nc.vector.scalar_tensor_tensor(second, hot1, -3.0e38, logit, ALU.mult, ALU.add))
                    link(nc.vector.tensor_reduce(m, src.rearrange("p (t e) -> p t e", t=NT), AX, ALU.max))
                    for t in range(NT):
                        o = EXPERTS * t
                        ins = nc.vector.scalar_tensor_tensor(key[:, o:o + EXPERTS], src[:, o:o + EXPERTS], m[:, t:t + 1],
                                                             down, ALU.is_equal, ALU.mult)
                        if t == 0:
                            ins.then_inc(dve_step, 1)
                            step[0] += 1
                    link(ins)
                    link(nc.vector.tensor_reduce(r, key.rearrange("p (t e) -> p t e", t=NT), AX, ALU.max))
                    for t in range(NT):
                        o = EXPERTS * t
                        link(nc.vector.tensor_scalar(hot[:, o:o + EXPERTS], down, r[:, t:t + 1], None, ALU.is_equal))
                nc.vector.tensor_tensor(gdiff, m2, m1, ALU.subtract).then_inc(gdiff_sb, 1)
                nc.vector.tensor_tensor(chosen, hot1, hot2, ALU.add).then_inc(chosen_sb, 1)
                for t in range(NT):
                    o = t * D
                    rest(xn_lo[:, o:o + D], h[:, o:o + D], xn_hi[:, o:o + D], xn_h, t + 1, xn_ready)
                dve.wait_ge(gexp_sb, 1)
                link(nc.vector.tensor_scalar(g1, gexp, 1.0, None, ALU.add))
                link(nc.vector.reciprocal(g1, g1))
                link(nc.vector.tensor_tensor(g2, gexp, g1, ALU.mult))
                for t in range(NT):
                    o = EXPERTS * t
                    link(nc.vector.tensor_scalar(hot2[:, o:o + EXPERTS], hot2[:, o:o + EXPERTS], g2[:, t:t + 1], None,
                                                 ALU.mult))
                for t in range(NT):
                    o = EXPERTS * t
                    link(nc.vector.scalar_tensor_tensor(gates[:, o:o + EXPERTS], hot1[:, o:o + EXPERTS], g1[:, t:t + 1],
                                                        hot2[:, o:o + EXPERTS], ALU.mult, ALU.add))
                dve.wait_ge(place_ps, 1)
                dve.wait_ge(chosen_sb, 1)
                link(nc.vector.tensor_tensor(place1, chosen, bank[5][:, 0:16], ALU.mult))
                link(nc.vector.tensor_reduce(most, bank[5][:, 16:24], AX, ALU.max))
                link(nc.vector.tensor_scalar(place1, place1, -1.0, None, ALU.add))
                link(nc.vector.tensor_scalar(place2, place1, -float(CAP), None, ALU.add))
                nc.vector.tensor_copy(most_int[:, 0:1], most).then_inc(count_sb, 1)
                nc.vector.memset(small2[:, 53:54], 0.0).then_inc(added, 1)

            def picks(sweep, e, v):
                dve.wait_ge(pickT_ps, v)
                where = (place1, place2)[sweep]
                for t in range(NT):
                    nc.vector.tensor_scalar(pick[:, t * P:(t + 1) * P], consts[:, K_IOTA:K_IOTA + P],
                                            where[:, ds(e + EXPERTS * t, 1)], None, ALU.is_equal).then_inc(pick_sb, 1)

            def gathered(v):
                for j in range(2):
                    rest(xe_lo[:, 512 * j:512 * (j + 1)], bank[6 + j][:], xe_hi[:, 512 * j:512 * (j + 1)],
                         xe_h, v + j + 1, xe_ready)

            def e_mult(c, u, t):
                dve.wait_ge(e_silu, u + c + 1)
                dve.wait_ge(block_used, expert_block(t, 6 * c + 2 if c else 4))
                nc.vector.tensor_tensor(gate_out[c % 2][:], gate_out[c % 2][:], bank[2 * (c % 2) + 1][:],
                                        ALU.mult).then_inc(e_g, 1)

            def e_gT_rest(c, u):
                rest(e_gT_lo[:], bank[2 * (c % 2)][:], e_gT_hi[:], e_gT_h, u + c + 1, e_gT)

            def expert(sweep, e, turn=0, last=False):
                t_ = turn + (EXPERTS * sweep + e)
                u = t_ * CHUNKS

                def sp_(k):
                    split(MOE0 + k, t_, PER_EXPERT)

                for k in range(4, 8):
                    sp_(k)
                for c in range(1, CHUNKS):
                    e_mult(c - 1, u, t_)
                    sp_(6 * c + 2)
                    sp_(6 * c + 3)
                    e_gT_rest(c - 1, u)
                    if c == 3 and not last:
                        picks(sweep, turn + (e + 1), t_ + 1)
                    if c < CHUNKS - 1:
                        for k in range(4):
                            sp_(6 * c + 4 + k)
                    else:
                        for k in range(2 if last else 4):
                            sp_(40 + k)
                e_mult(CHUNKS - 1, u, t_)
                if not last:
                    gathered(t_ * 2 + 2)
                e_gT_rest(CHUNKS - 1, u)
                if not last:
                    sp_(44)
                    sp_(45)
                for j in range(2):
                    rest(y_lo[:, 512 * j:512 * (j + 1)], bank[4 + j][:], y_hi[:, 512 * j:512 * (j + 1)],
                         y_h, t_ * 2 + j + 1, y_ready)
                for t in range(NT):
                    for j in range(2):
                        dve.wait_ge(back_ps, t_ * 4 + (2 * t + j + 1))
                        o = D * t + 512 * j
                        nxt = nc.vector.scalar_tensor_tensor(x[:, o:o + 512], bank[(6, 4)[t] + j][:],
                                                       gates[:, ds(turn + (e + EXPERTS * t), 1)], x[:, o:o + 512],
                                                       ALU.mult, ALU.add)
                nxt.then_inc(added, 1)
                dve.wait_ge(added, t_ + 2)

            def sweep_experts(sweep):
                if sweep:
                    for k in range(4):
                        split(MOE0 + k, EXPERTS * sweep, PER_EXPERT)
                picks(sweep, 0, EXPERTS * sweep) if sweep else picks0()
                gathered(2 * EXPERTS * sweep)
                with dve.Fori(0, EXPERTS - 1) as e:
                    expert(sweep, 0, turn=e)
                expert(sweep, EXPERTS - 1, last=True)

            def picks0():
                for t in range(NT):
                    nc.vector.tensor_scalar(pick[:, t * P:(t + 1) * P], consts[:, K_IOTA:K_IOTA + P],
                                            place1[:, EXPERTS * t:EXPERTS * t + 1], None,
                                            ALU.is_equal).then_inc(pick_sb, 1)

            nc.vector.memset(ones[:], 1.0).then_inc(ones_set, 1)
            nc.vector.memset(w_gate[0:32, :], 0.0).then_inc(ones_set, 1)
            ones_row(0)
            nc.vector.memset(setup_wide[REL_BUCKETS:REL_BUCKETS + 1, :], 1.0).then_inc(rel_set, 1)
            dve.wait_ge(hot_loaded, 32)
            nc.vector.tensor_copy(setup_wide[0:REL_BUCKETS, :].rearrange("p (h m) -> p h m", h=NH),
                                  setup_rel[0:REL_BUCKETS, 0:NH].rearrange("p (h m) -> p h m", m=1)
                                  .broadcast_to([REL_BUCKETS, NH, P])).then_inc(rel_set, 1)
            for i in range(NH):
                dve.wait_ge(bias_ps, i + 1)
                nc.vector.tensor_copy(setup_bias[:, 512 * i:512 * (i + 1)], bank[4 + i][:]).then_inc(bias_sb, 1)
            for k in range(3):
                split(k)
            dve.wait_ge(router_split, 1)
            nc.vector.tensor_tensor(router_lo[:], setup_router[:], router_hi[:].bitcast(F32),
                                    ALU.subtract).then_inc(router_split, 1)
            for k in range(3, 6):
                split(k)
            dve.wait_ge(params_loaded, 64)
            nc.vector.tensor_copy(masks[:], setup_masks[:]).then_inc(masks_set, 1)
            mixer(0)
            norm_rows(1)
            turn_lo(1)
            dense_chunk(0)
            dense_chunk(1)
            with dve.Fori(0, DENSE_FULL - 3) as c:
                dense_chunk(2, c)
            dense_chunk(DENSE_FULL - 1)
            dense_chunk(DENSE_FULL)
            dve.wait_ge(x_ready, 2)
            ones_row(1)
            mixer(1)
            norm_rows(3)
            turn_lo(3)
            route()
            sweep_experts(0)
            dve.wait_ge(count_sb, 1)
            count = dve.value_load(most_int[0:1, 0:1], min_val=0, max_val=SEQ)
            with dve.If(count > CAP):
                sweep_experts(1)
            nc.vector.tensor_copy(small2[:, 52:53], x[:, 0:1]).then_inc(x_ready, 1)
            norm_rows(4)

        @block.tensor
        def _(pe):
            mm = nc.tensor.matmul

            def split3(dst, a_hi, a_lo, b_hi, b_lo, start, stop):
                mm(dst, a_hi, b_hi, start=start, stop=False)
                mm(dst, a_hi, b_lo, start=False, stop=False)
                return mm(dst, a_lo, b_hi, start=False, stop=stop)

            def weights(n, k, cols, c0, c1):
                w = n % SLOTS
                return (whi[w][:, k * cols + c0:k * cols + c1], wlo[w][:, k * cols + c0:k * cols + c1])

            def rows(k, t):
                o = k * SEQ + t * P
                return f_hi[:, o:o + P], f_lo[:, o:o + P]

            def feats(k):
                return f_hi[:, k * SEQ:(k + 1) * SEQ], f_lo[:, k * SEQ:(k + 1) * SEQ]

            def turn_rows(i):
                pe.wait_ge(h_ready, 2 * i + 2)
                for j in range(4):
                    for q in range(4):
                        k, t = 2 * j + q // 2, q % 2
                        ins = pe.transpose(bank[j][:, q * P:(q + 1) * P], h[:, t * D + k * P:t * D + (k + 1) * P], ident())
                    ins.then_inc(hT_ps, 1)
                pe.wait_ge(hT_ready, 4 * i + 4)

            def by_feature(blocks, cols, outs):
                ks = [(n, k) for n, nk in blocks for k in range(nk)]
                pe.wait_ge(lo_ready, blocks[-1][0] + 1)
                for i, (bk, at_, c, signal) in enumerate(outs):
                    for j, (n, k) in enumerate(ks):
                        w_hi, w_lo = weights(n, k, cols, c, c + P)
                        f_h, f_l = feats(j)
                        ins = split3(bank[bk][:, at_:at_ + SEQ], w_hi, w_lo, f_h, f_l, j == 0, j == len(ks) - 1)
                        if i == len(outs) - 1 and k == dict(blocks)[n] - 1:
                            ins.then_inc(block_used, 1)
                    if signal is not None:
                        ins.then_inc(signal, 1)

            def by_token(blocks, cols, outs, signal):
                ks = [(n, k) for n, nk in blocks for k in range(nk)]
                pe.wait_ge(lo_ready, blocks[-1][0] + 1)
                for t, (bk, at_) in enumerate(outs):
                    for j, (n, k) in enumerate(ks):
                        w_hi, w_lo = weights(n, k, cols, 0, cols)
                        f_h, f_l = rows(j, t)
                        ins = split3(bank[bk][:, at_:at_ + cols], f_h, f_l, w_hi, w_lo, j == 0, j == len(ks) - 1)
                        if t == NT - 1 and k == dict(blocks)[n] - 1:
                            ins.then_inc(block_used, 1)
                    if t == 0 and signal is not None:
                        ins.then_inc(signal, 1)

            def head(i):
                return 64 * (i % 2), i // 2

            def mixer(l):
                b = BASE[l]
                turn_rows(2 * l)
                by_feature([(b, 4), (b + 1, 4)], 512,
                           [(0, 0, 0, None), (0, SEQ, P, q_ps), (1, 0, 2 * P, None), (1, SEQ, 3 * P, None)])
                by_feature([(b + 2, 4), (b + 3, 4)], 272,
                           [(2, 0, 0, glr_ps), (3, 0, RANK, None), (3, SEQ, RANK + P, None)])
                by_feature([(b + 4, 4), (b + 5, 4)], 512,
                           [(4, 0, 0, None), (4, SEQ, P, gq_ps), (5, 0, 2 * P, None), (5, SEQ, 3 * P, None)])
                pe.wait_ge(glr_sb, l + 1)
                pe.wait_ge(gate_loaded, 32 * (l + 1))
                for t in range(NT):
                    ins = mm(bank[7][:, 256 * t:256 * (t + 1)], glr[0:32, t * P:(t + 1) * P], w_gate[0:32, 0:256],
                             start=True, stop=True)
                ins.then_inc(z_ps, 1)
                by_token([(b + 6, 8)], 256, [(6, 0), (6, 256)], None)
                pe.wait_ge(qk_sb, 2 * l + 2)
                pe.wait_ge(cin_sb, l + 1)
                for t in range(NT):
                    n = P * (t + 1)
                    for i in range(NH):
                        off, pr = head(i)
                        bk = ((0, 3), (1, 2))[t][i % 2]
                        ins = mm(bank[bk][:, pr * n:(pr + 1) * n], qT[off:off + HD, pr * SEQ + t * P:pr * SEQ + (t + 1) * P],
                                 kT[off:off + HD, pr * SEQ:pr * SEQ + n], start=True, stop=True)
                        if pr == 1:
                            ins.then_inc(att_ps, 1)

                def decay_sums(i):
                    for pr in range(2):
                        for t in range(NT):
                            m = lev(i) if i < LEVELS else lev(LEVELS + t)
                            ins = mm(bank[(4, 7)[i % 2]][:, pr * SEQ + t * P:pr * SEQ + (t + 1) * P],
                                     log_a[:, t * 256 + pr * P:t * 256 + (pr + 1) * P], m, start=True, stop=True)
                    ins.then_inc(e_ps, 1)

                pe.wait_ge(log_ready, l + 1)
                pe.wait_ge(gqk_sb, 2 * l + 2)
                decay_sums(0)
                decay_sums(1)
                pe.wait_ge(av_sb, l + 1)
                by_token([(b + 7, 4), (b + 8, 4)], 512, [(5, 0), (6, 0)], gv_ps)
                for t in range(NT):
                    pe.wait_ge(prob_ready, 2 * l + t + 1)
                    for s in range(t + 1):
                        for i in range(NH):
                            n = P * (t + 1)
                            ins = pe.transpose(bank[t + s][:, i * P:(i + 1) * P],
                                               (prob0, prob1)[t][:, i * n + s * P:i * n + (s + 1) * P], ident())
                        ins.then_inc(pT_ps, 1)
                pe.wait_ge(gv_sb, 2 * l + 1)
                by_token([(b + 9, 4), (b + 10, 4)], 512, [(3, 0), (5, 0)], gr_ps)
                pe.wait_ge(pT_sb, 3 * l + 3)
                for i in range(NH):
                    off, pr = head(i)

                    def values(s):
                        return av[:, s * 256 + i * HD:s * 256 + (i + 1) * HD]

                    o = bank[0][off:off + HD, pr * SEQ:(pr + 1) * SEQ]
                    mm(o[:, 0:P], values(0), pT[:, i * P:(i + 1) * P], start=True, stop=True)
                    mm(o[:, P:SEQ], values(0), pT[:, 512 + i * P:512 + (i + 1) * P], start=True, stop=False)
                    ins = mm(o[:, P:SEQ], values(1), pT[:, 1024 + i * P:1024 + (i + 1) * P], start=False, stop=True)
                ins.then_inc(atto_ps, 1)

                def level(i):
                    if i < 0:
                        q, k = gqT[:], gkT[:]
                        pe.wait_ge(gr_sb, 2 * l + 2)
                        pe.wait_ge(gv_sb, 2 * l + 2)
                    else:
                        off_ = 1024 * (i % 2)
                        q, k = qk_level[:, off_:off_ + 512], qk_level[:, off_ + 512:off_ + 1024]
                        pe.wait_ge(level_sb, 8 * l + i + 1)
                        pe.wait_ge(s_sb, 18 * l + 2 * (i + 1))
                    last = [None, None]
                    for pr in range(2):
                        for t in range(NT if i < LEVELS else 1):
                            for odd in range(2):
                                off = 64 * odd
                                g = pr * NT + t if i < LEVELS else pr
                                tq = t if i < LEVELS else 1
                                o = pr * SEQ
                                last[odd] = ins = mm(bank[5 + odd][:, g * P:(g + 1) * P],
                                                     k[off:off + HD, o + t * P:o + (t + 1) * P],
                                                     q[off:off + HD, o + tq * P:o + (tq + 1) * P], start=True, stop=True)
                                if g == (3 if i < LEVELS else 1):
                                    ins.then_inc(s_ps, 1)

                level(-1)
                level(0)
                decay_sums(2)
                by_feature([(b + 11, 4), (b + 12, 4)], 512,
                           [(1, 0, 0, None), (1, SEQ, P, None), (2, 0, 2 * P, None), (2, SEQ, 3 * P, None)])
                for i in range(1, LEVELS + 1):
                    level(i)
                    if i + 2 <= LEVELS:
                        decay_sums(i + 2)
                pe.wait_ge(s_sb, 18 * (l + 1))
                for t in range(NT):
                    for i in range(NH):
                        odd, pr = i % 2, i // 2
                        o = bank[3 + t][:, i * P:(i + 1) * P]

                        def inside(s):
                            a = 512 * odd + (pr * NT + s) * P
                            return scores[:, a:a + P]

                        if t:
                            mm(o, cross[:, 256 * odd + pr * P:256 * odd + (pr + 1) * P], gv[:, i * DV:(i + 1) * DV],
                               start=True, stop=False)
                        ins = mm(o, inside(t), gv[:, t * 512 + i * DV:t * 512 + (i + 1) * DV], start=t == 0, stop=True)
                    ins.then_inc(o_ps, 1)
                pe.wait_ge(go_sb, l + 1)
                for j in range(2):
                    for q in range(4):
                        i, t = 2 * j + q // 2, q % 2
                        ins = pe.transpose(bank[5 + j][:, q * P:(q + 1) * P],
                                           go[:, (NH * t + i) * P:(NH * t + i + 1) * P], ident())
                    ins.then_inc(go_ps, 1)
                for j in range(4):
                    n = b + N_IN + j
                    pe.wait_ge(mix_ready, 4 * l + j + 1)
                    pe.wait_ge(lo_ready, n + 1)
                    if j == 0:
                        pe.wait_ge(mix_ready, 4 * l + 2)
                    for k in range(2):
                        for t in range(NT):
                            for half in range(2):
                                w_hi, w_lo = weights(n, k, D, 512 * half, 512 * (half + 1))
                                f_h, f_l = rows(2 * j + k, t)
                                ins = split3(bank[(0, 1, 2, 7)[2 * t + half]][:], f_h, f_l, w_hi, w_lo,
                                             j == 0 and k == 0, j == 3 and k == 1)
                    ins.then_inc(block_used, 1)

            def up(bk, f, blocks, width, waits, signal):
                for s, v in waits:
                    pe.wait_ge(s, v)
                j = 0
                total = sum(nk for _, nk, _ in blocks)
                for w, nk, v in blocks:
                    pe.wait_ge(lo_ready, v)
                    for k in range(nk):
                        f_h, f_l = f(j)
                        w_hi, w_lo = (x_[w][:, k * width:(k + 1) * width] for x_ in (whi, wlo))
                        ins = split3(bank[bk][:, 0:width], f_h, f_l, w_hi, w_lo, j == 0, j == total - 1)
                        j += 1
                    if signal is None:
                        ins.then_inc(block_used, 1)
                if signal is not None:
                    ins.then_inc(signal, 1)

            def turn_gate(src, bk, width, ready, v, signal):
                pe.wait_ge(ready, v)
                for q in range(width // P):
                    ins = pe.transpose(bank[bk][:, q * P:(q + 1) * P], src[:, q * P:(q + 1) * P], ident())
                ins.then_inc(signal, 1)

            def down(y0, g_h, g_l, blocks, first, final, ready, v, signal):
                pe.wait_ge(ready, v)
                k0 = 0
                for i, (w, v_) in enumerate(blocks):
                    pe.wait_ge(lo_ready, v_)
                    for k in range(2):
                        for half in range(2):
                            o = k * D + 512 * half
                            ins = split3(bank[y0 + half][:], g_h[:, k0 * P:(k0 + 1) * P], g_l[:, k0 * P:(k0 + 1) * P],
                                         whi[w][:, o:o + 512], wlo[w][:, o:o + 512],
                                         first and k0 == 0, final and i == len(blocks) - 1 and k == 1)
                        k0 += 1
                    if signal is None:
                        ins.then_inc(block_used, 1)
                if signal is not None:
                    ins.then_inc(signal, 1)

            def dense_up(c, t, i, turn=0):
                n = DENSE0 + 6 * c + 2 * i
                if c < DENSE_FULL:
                    blocks = [((n + k) % SLOTS, 4, 6 * turn + n + k + 1) for k in range(2)]
                    width = FC
                else:
                    n = DENSE0 + 6 * c + i
                    blocks = [(n % SLOTS, 8, n + 1)]
                    width = HALF
                up(2 * t + i, lambda j: rows(j, t), blocks, width, [], (h1_ps, h3_ps)[i] if t == 0 else None)

            def dense_turn(c, t, turn=0):
                turn_gate(gate_out[t], 2 * t, FC if c < DENSE_FULL else HALF, g_ready, 2 * turn + 2 * c + t + 1, gT_ps)

            def dense_down(c, t, turn=0):
                n = DENSE0 + 6 * c + 4
                if c < DENSE_FULL:
                    blocks = [((n + k) % SLOTS, 6 * turn + n + k + 1) for k in range(2)]
                else:
                    n = DENSE0 + 6 * c + 2
                    blocks = [(n % SLOTS, n + 1)]
                down(4 + 2 * t, gT_hi[t], gT_lo[t], blocks, c == 0, c == DENSE_FULL, gT_ready,
                     2 * turn + 2 * c + t + 1, y_ps if t == 0 else None)

            def dense_chunk(c, turn=0):
                dense_up(c, 0, 0, turn)
                if c:
                    dense_turn(c - 1, 1, turn)
                dense_up(c, 0, 1, turn)
                if c:
                    dense_down(c - 1, 1, turn)
                dense_up(c, 1, 0, turn)
                dense_turn(c, 0, turn)
                dense_up(c, 1, 1, turn)
                dense_down(c, 0, turn)

            def gather(v):
                pe.wait_ge(pick_sb, v * 2 + 2)
                for k in range(KD):
                    o = bank[6 + k // 4][:, (k % 4) * P:(k % 4 + 1) * P]
                    for t in range(NT):
                        a = t * D + k * P
                        mm(o, xn_hi[:, a:a + P], pick[:, t * P:(t + 1) * P], start=t == 0, stop=False)
                        ins = mm(o, xn_lo[:, a:a + P], pick[:, t * P:(t + 1) * P], start=False, stop=t == NT - 1)
                    if k % 4 == 3:
                        ins.then_inc(xe_ps, 1)

            def turn_pick():
                for t in range(NT):
                    ins = pe.transpose(bank[2][:, t * P:(t + 1) * P], pick[:, t * P:(t + 1) * P].bitcast(F32), ident())
                ins.then_inc(pickT_ps, 1)

            def expert(sweep, e, turn=0, last=False):
                t_ = turn + (EXPERTS * sweep + e)
                u = t_ * CHUNKS
                nb = t_ * PER_EXPERT

                def places(k):
                    return xe_hi[:, k * P:(k + 1) * P], xe_lo[:, k * P:(k + 1) * P]

                def pair(k):
                    return [((MOE0 + k + i) % SLOTS, nb + (MOE0 + k + i + 1)) for i in range(2)]

                def e_up(c, i):
                    k = (0, 2)[i] if c == 0 else 6 * c - 2 + 2 * i
                    waits = []
                    if c == 0 and i == 0:
                        waits.append((xe_ready, t_ * 2 + 2))
                    if c == 1 and i == 0:
                        waits.append((pickT_sb, t_ + 1))
                    up(2 * (c % 2) + i, places, [(w, 4, v) for w, v in pair(k)], FC, waits, None)

                def e_turn(c):
                    turn_gate(gate_out[c % 2], 2 * (c % 2), FC, e_g, u + c + 1, e_gT_ps)

                def e_down(c):
                    if c == 0:
                        pe.wait_ge(added, t_ + 1)
                    k = 6 * c + 8 if c < CHUNKS - 1 else 40
                    down(4, e_gT_hi, e_gT_lo, pair(k), c == 0, c == CHUNKS - 1, e_gT, u + c + 1, None)

                for c in range(CHUNKS):
                    e_up(c, 0)
                    if c:
                        e_turn(c - 1)
                    e_up(c, 1)
                    if c:
                        e_down(c - 1)
                if not last:
                    gather(t_ + 1)
                e_turn(CHUNKS - 1)
                e_down(CHUNKS - 1)
                pe.wait_ge(y_ready, t_ * 2 + 2)
                if not last:
                    pe.wait_ge(xe_ready, t_ * 2 + 4)
                for t in range(NT):
                    for j in range(2):
                        o = bank[(6, 4)[t] + j][:]
                        mm(o, pickT[:, t * P:(t + 1) * P], y_hi[:, 512 * j:512 * (j + 1)], start=True, stop=False)
                        mm(o, pickT[:, t * P:(t + 1) * P], y_lo[:, 512 * j:512 * (j + 1)], start=False,
                           stop=True).then_inc(back_ps, 1)
                if not last:
                    turn_pick()

            def sweep_experts(sweep):
                if sweep:
                    pe.wait_ge(added, EXPERTS * sweep + 1)
                gather(EXPERTS * sweep)
                turn_pick()
                with pe.Fori(0, EXPERTS - 1) as e:
                    expert(sweep, 0, turn=e)
                expert(sweep, EXPERTS - 1, last=True)

            pe.wait_ge(hot_loaded, 32)
            pe.wait_ge(rel_set, 2)
            for i in range(NH):
                mm(bank[4 + i][:], setup_wide[0:REL_BUCKETS + 1, i * P:(i + 1) * P], setup_hot[0:REL_BUCKETS + 1, :],
                   start=True, stop=True).then_inc(bias_ps, 1)
            pe.wait_ge(bias_sb, NH)
            pe.wait_ge(consts_loaded, 16)
            mixer(0)
            turn_rows(1)
            dense_chunk(0)
            dense_chunk(1)
            with pe.Fori(0, DENSE_FULL - 3) as c:
                dense_chunk(2, c)
            dense_chunk(DENSE_FULL - 1)
            dense_chunk(DENSE_FULL)
            dense_turn(DENSE_FULL, 1)
            dense_down(DENSE_FULL, 1)
            mixer(1)
            turn_rows(3)
            pe.wait_ge(router_split, 2)
            for t in range(NT):
                for k in range(KD):
                    f_h, f_l = rows(k, t)
                    ins = split3(bank[4][:, 8 * t:8 * t + 8], f_h, f_l, router_hi[:, 8 * k:8 * k + 8],
                                 router_lo[:, 8 * k:8 * k + 8], k == 0, k == KD - 1)
            ins.then_inc(logit_ps, 1)
            pe.wait_ge(chosen_sb, 1)
            until = lev(LEVELS + 1)
            mm(bank[5][:, 0:8], until, chosen[:, 0:8], start=True, stop=True)
            mm(bank[5][:, 8:16], ones[:], chosen[:, 0:8], start=True, stop=False)
            mm(bank[5][:, 8:16], until, chosen[:, 8:16], start=False, stop=True)
            mm(bank[5][:, 16:24], ones[:], chosen[:, 0:8], start=True, stop=False)
            mm(bank[5][:, 16:24], ones[:], chosen[:, 8:16], start=False, stop=True).then_inc(place_ps, 1)
            pe.wait_ge(xn_ready, 2)
            pe.wait_ge(count_sb, 1)
            sweep_experts(0)
            count = pe.value_load(most_int[0:1, 0:1], min_val=0, max_val=SEQ)
            with pe.If(count > CAP):
                sweep_experts(1)


_OUT_SHAPE = (1, SEQ, D)


def kernel(x, w_mix_in, w_mix_out, g_mix, rel_bias, gla_w_gate, gla_b_gate, gla_g_norm, conv_w, g_ffn,
           ffn_w1, ffn_w3, ffn_w2, moe_router, moe_w1, moe_w3, moe_w2, g_final):
    import concourse.bacc as bacc
    from concourse.bass_utils import run_bass_kernel_spmd

    given = dict(x=x, w_mix_in=w_mix_in, w_mix_out=w_mix_out, g_mix=g_mix, rel_bias=rel_bias, gla_w_gate=gla_w_gate,
                 gla_b_gate=gla_b_gate, gla_g_norm=gla_g_norm, conv_w=conv_w, g_ffn=g_ffn, ffn_w1=ffn_w1,
                 ffn_w3=ffn_w3, ffn_w2=ffn_w2, moe_router=moe_router, moe_w1=moe_w1, moe_w3=moe_w3, moe_w2=moe_w2,
                 g_final=g_final)
    taps = np.asarray(conv_w).reshape(DEPTH, 3, 2, P).transpose(3, 0, 2, 1).reshape(P, DEPTH * 6)
    given.update(conv_w=taps, gla_g_norm=np.asarray(gla_g_norm).T)
    c, m, o = shape_constants()
    given.update(shape_consts=c, shape_masks=m, shape_buckets=o)
    nc = bacc.Bacc("TRN2", target_bir_lowering=False, num_devices=1)
    arrays, args = {}, []
    for name, a in given.items():
        a = np.ascontiguousarray(a)
        arrays[f"in_{name}"] = a
        args.append(nc.dram_tensor(f"in_{name}", a.shape, mybir.dt.from_np(a.dtype), kind="ExternalInput").ap())
    args.append(nc.dram_tensor("out_0", _OUT_SHAPE, F32, kind="ExternalOutput").ap())
    trunk(nc, *args)
    r = run_bass_kernel_spmd(nc, [arrays], core_ids=[0])
    return r.results[0]["out_0"]
```

```python
from contextlib import ExitStack

import numpy as np

import concourse.bass as bass
from concourse import mybir

F32 = mybir.dt.float32
F32R = mybir.dt.float32r
I32 = mybir.dt.int32
U8 = mybir.dt.uint8
ALU = mybir.AluOpType
ACT = mybir.ActivationFunctionType
AX = mybir.AxisListType.X
ds = bass.ds

P = 128
D = 1024
SEQ = 256
NT = SEQ // P
KD = D // P
EPS = 1e-6
DEPTH = 2
HD = 64
NH = 4
DV = 128
RANK = 16
CONV = 256
EXPERTS = 8
F_DENSE = 2816
F_EXPERT = 3584
FC = 512
BLOCK = 2048
LEVELS = 7
CAP = P
FAR = -1.0e30
DILATED_PATTERNS = ((128, 1), (512, 4), (2048, 16))
REL_BUCKETS = 32
REL_MAX_DISTANCE = 2048

C_AQ, C_AK, C_AV = 0, 256, 512
C_GQ, C_GK, C_GV, C_GR = 768, 1024, 1280, 1792
C_LR, C_IN, C_B, C_C = 2304, 2320, 2576, 2832

MIX_IN = [(C_AV, 256, 0, 8),
          (C_GR, 512, 0, 4), (C_GR, 512, 4, 4),
          (C_LR, 272, 0, 4), (C_LR, 272, 4, 4),
          (C_AQ, 512, 0, 4), (C_AQ, 512, 4, 4),
          (C_GQ, 512, 0, 4), (C_GQ, 512, 4, 4),
          (C_GV, 512, 0, 4), (C_GV, 512, 4, 4),
          (C_B, 512, 0, 4), (C_B, 512, 4, 4)]
OUT_ROWS = [0, 768, 256, 512]
N_IN = len(MIX_IN)
N_MIX = N_IN + len(OUT_ROWS)
DENSE_FULL = F_DENSE // FC
HALF = F_DENSE - DENSE_FULL * FC
N_DENSE_BLOCKS = 6 * DENSE_FULL + 3
BASE = [0, N_MIX + N_DENSE_BLOCKS]
DENSE0 = N_MIX
MOE0 = BASE[1] + N_MIX
CHUNKS = F_EXPERT // FC
PER_EXPERT = 6 * CHUNKS
SLOTS = 6
RAW_FIXED = 3

K_ID, K_LEV, K_IOTA, K_DOWN = 0, P, P + 9 * P, P + 10 * P
K_COLS = K_DOWN + 16


def block_size(n):
    m = n - BASE[1] if n >= BASE[1] else n
    if m < N_IN:
        return MIX_IN[m][1] * MIX_IN[m][3]
    return BLOCK


def raw_plan():
    slot, use, before, count, last = {}, {}, {}, [0] * SLOTS, [None] * SLOTS
    for n in range(MOE0 + 2 * PER_EXPERT):
        m = n - BASE[1] if n >= BASE[1] else n
        s = (m + 1) % RAW_FIXED if m < N_MIX else (m - N_MIX) % SLOTS
        slot[n], before[n] = s, last[s]
        count[s] += 1
        use[n], last[s] = count[s], n
    return slot, use, before


def shape_constants():
    c = np.zeros((P, K_COLS), np.float32)
    c[:, K_ID:K_ID + P] = np.eye(P)
    s, t = np.meshgrid(np.arange(P), np.arange(P), indexing="ij")
    masks = np.zeros((P, LEVELS * P), np.int32)
    for level in range(LEVELS):
        half = 1 << level
        mid = t // (2 * half) * (2 * half) + half
        between = np.where(t >= mid, (s >= mid) & (s <= t), (s > t) & (s < mid))
        c[:, K_LEV + level * P:K_LEV + (level + 1) * P] = between
        masks[:, level * P:(level + 1) * P] = (s // (2 * half) == t // (2 * half)) & (s < mid) & (t >= mid)
    c[:, K_LEV + 7 * P:K_LEV + 8 * P] = s > t
    c[:, K_LEV + 8 * P:K_LEV + 9 * P] = s <= t
    c[:, K_IOTA:K_IOTA + P] = np.arange(P)
    c[:, K_DOWN:K_DOWN + 16] = np.tile(np.arange(EXPERTS, 0, -1), 2)
    onehot = np.zeros((REL_BUCKETS + 1, 512), np.float32)
    dist = 255 - np.arange(512)
    exact = REL_BUCKETS // 2
    d = np.maximum(dist, 0)
    ratio = np.log(np.maximum(d, 1).astype(np.float32) / exact) / np.float32(np.log(REL_MAX_DISTANCE / exact))
    large = np.minimum(exact + (ratio * (REL_BUCKETS - exact)).astype(np.int32), REL_BUCKETS - 1)
    onehot[np.where(d < exact, d, large), np.arange(512)] = 1.0
    held = sum(((dist >= 0) & (dist % dil == 0) & (dist // dil <= win // dil)).astype(np.int32)
               for win, dil in DILATED_PATTERNS)
    onehot[REL_BUCKETS] = np.where(held > 0, np.log(np.maximum(held, 1)), FAR)
    return c, masks, onehot


def trunk(nc, x_in, w_mix_in, w_mix_out, g_mix, rel_bias, gla_w_gate, gla_b_gate, gla_g_norm, conv_w,
          g_ffn, ffn_w1, ffn_w3, ffn_w2, moe_router, moe_w1, moe_w3, moe_w2, g_final,
          consts_in, masks_in, onehot_in, out):
    raw_slot, raw_use, raw_before = raw_plan()
    ctx = ExitStack()
    with ctx:
        at = [(nc.sbuf_base + 31) // 32 * 32]

        def place(name, cols, dt=F32, offset=None):
            size = 1 if dt == U8 else 4
            where = at[0] if offset is None else offset
            t = nc.alloc_sbuf_tensor_at(name, [P, cols], dt, offset=where)
            if offset is None:
                at[0] += (cols * size + 31) // 32 * 32
            return t

        raw = [place(f"raw{i}", BLOCK) for i in range(RAW_FIXED)]
        whi = [place(f"whi{i}", BLOCK, F32R) for i in range(SLOTS)]
        wlo = [place(f"wlo{i}", BLOCK, F32R) for i in range(SLOTS)]
        x = place("x", NT * D)
        h_at = at[0]
        h = place("h", NT * D)
        f_at = at[0]
        f_hi = place("f_hi", KD * SEQ, F32R)
        f_lo = place("f_lo", KD * SEQ, F32R)
        consts = place("consts", K_COLS)
        masks = place("masks", LEVELS * P, U8)
        small = place("small", 224)
        router_hi = place("router_hi", 64, F32R)
        router_lo = place("router_lo", 64, F32R)
        arena = at[0]

        gv = place("gv", NT * NH * DV, offset=h_at)
        gr = place("gr", NT * NH * DV, offset=h_at + 4096)
        g_row = place("g_row", D)
        ffn_arena = at[0]
        qT = place("qT", 512)
        kT = place("kT", 512)
        pt_tail = place("pt_tail", 512)
        av = place("av", 512)
        bias0 = place("bias0", NH * P)
        bias1 = place("bias1", NH * 2 * P)
        qk_tail = place("qk_tail", 512)
        prob0 = place("prob0", NH * P)
        prob1 = place("prob1", NH * 2 * P)
        gqT = place("gqT", 512)
        gkT = place("gkT", 512)
        log_a = place("log_a", 512)
        decay = place("decay", 512)
        scores = place("scores", 1024)
        cross = place("cross", 512)
        cin = place("cin", 512)
        cy = place("cy", 512)
        glr = place("glr", 256)
        w_gate = place("w_gate", 512)
        mix_end = at[0]
        base = {t: o for t, o in (("qT", ffn_arena), ("bias0", ffn_arena + 4 * 2048))}
        pT = place("pT", 1536, offset=base["qT"])
        qk_level = place("qk_level", 2048, offset=base["bias0"])
        go = place("go", 1024, offset=base["bias0"] + 4 * 2048)
        z_a = place("z_a", 512, offset=base["bias0"] + 4 * 2048 + 3 * 2048 + 4 * 2048)
        z_b = place("z_b", 512, offset=base["bias0"] + 4 * 2048 + 3 * 2048 + 5 * 2048)
        setup_hot = place("setup_hot", 512, offset=base["bias0"] + 4 * 2048)
        setup_rel = place("setup_rel", 8, offset=base["bias0"] + 5 * 2048)
        setup_wide = place("setup_wide", NH * P, offset=base["bias0"] + 6 * 2048)
        setup_bias = place("setup_bias", NH * 512, offset=base["bias0"] + 4 * 2048 + 3 * 2048)
        setup_masks = place("setup_masks", LEVELS * P, I32, offset=base["bias0"] + 4 * 2048 + 3 * 2048 + 4 * 2048)
        setup_router = place("setup_router", 64, offset=base["bias0"] + 5 * 2048 + 256)

        at[0] = ffn_arena
        raw += [place(f"raw{i}", BLOCK) for i in range(RAW_FIXED, SLOTS)]
        gate_out = [place(f"gate_out{i}", FC) for i in range(2)]
        gT_at = at[0]
        gT_hi = [place(f"gT_hi{i}", FC, F32R) for i in range(2)]
        gT_lo = [place(f"gT_lo{i}", FC, F32R) for i in range(2)]
        dense_end = at[0]
        at[0] = gT_at + 2 * 4 * FC
        e_gT_hi = gT_hi[0]
        e_gT_lo = place("e_gT_lo", FC, F32R, offset=gT_at + 4 * FC)
        xe_hi = place("xe_hi", KD * P, F32R)
        xe_lo = place("xe_lo", KD * P, F32R)
        pick = place("pick", NT * P, F32R)
        pickT = place("pickT", NT * P, F32R)
        moe_end = at[0]
        assert max(mix_end, dense_end, moe_end) <= nc.sbuf_usable_end, (mix_end, dense_end, moe_end)
        xn_hi = place("xn_hi", NT * D, F32R, offset=f_at)
        xn_lo = place("xn_lo", NT * D, F32R, offset=f_at + 4 * NT * D)
        y_hi = place("y_hi", D, F32R, offset=h_at)
        y_lo = place("y_lo", D, F32R, offset=h_at + 4 * D)

        sq, ms, rs = small[:, 0:2], small[:, 2:4], small[:, 4:6]
        sq8, ms8, rs8 = small[:, 8:16], small[:, 16:24], small[:, 24:32]
        top, neg, rsum, rinv = small[:, 32:40], small[:, 40:48], small[:, 48:56], small[:, 56:64]
        power = small[:, 64:72]
        conv_k = small[:, 72:84]
        gnorm = small[:, 84:86]
        logit = small[:, 88:104]
        hot1, hot2, key, second = small[:, 104:120], small[:, 120:136], small[:, 136:152], small[:, 152:168]
        m1, m2, r1, r2 = small[:, 168:170], small[:, 170:172], small[:, 172:174], small[:, 174:176]
        gdiff, gexp, g1, g2 = small[:, 176:178], small[:, 178:180], small[:, 180:182], small[:, 182:184]
        chosen = small[:, 184:200]
        small2 = nc.alloc_sbuf_tensor_at("small2", [P, 64], F32, offset=max(mix_end, dense_end, moe_end))
        assert max(mix_end, dense_end, moe_end) + 64 * 4 + 512 + 64 <= nc.sbuf_usable_end
        gates, place1, place2, most = small2[:, 0:16], small2[:, 16:32], small2[:, 32:48], small2[:, 48:49]
        most_int = nc.alloc_sbuf_tensor_at("most_int", [P, 8], I32, offset=max(mix_end, dense_end, moe_end) + 256)
        ones = nc.alloc_sbuf_tensor_at("ones", [P, P], F32, offset=max(mix_end, dense_end, moe_end) + 288)

        bank = [ctx.enter_context(nc.psum_tensor(f"bank{i}", [P, 512], F32)) for i in range(8)]
        bias_dram = nc.dram_tensor("bias_by_distance", [P, NH * 512], F32).ap()

        def sem(name):
            return ctx.enter_context(nc.semaphore(name))

        raw_full = [sem(f"raw_full{i}") for i in range(SLOTS)]
        hi_ready, lo_ready, block_used = sem("hi_ready"), sem("lo_ready"), sem("block_used")
        x_loaded = [sem(f"x_loaded{t}") for t in range(NT)]
        consts_loaded, tables_loaded, params_loaded = sem("consts_loaded"), sem("tables_loaded"), sem("params_loaded")
        hot_loaded, first_gains, gains_loaded = sem("hot_loaded"), sem("first_gains"), sem("gains_loaded")
        gate_loaded = sem("gate_loaded")
        bias_ps, bias_sb, bias_stored, bias_loaded = (sem(n) for n in ("bias_ps", "bias_sb", "bias_stored", "bias_loaded"))
        ones_set, power_set, router_split = sem("ones_set"), sem("power_set"), sem("router_split")
        masks_set, c_ps = sem("masks_set"), sem("c_ps")
        x_ready, squares, means, roots, h_ready = (sem(n) for n in ("x_ready", "squares", "means", "roots", "h_ready"))
        hT_ps, hT_hi, hT_ready = sem("hT_ps"), sem("hT_hi"), sem("hT_ready")
        q_ps, glr_ps, gq_ps, z_ps = (sem(n) for n in ("q_ps", "glr_ps", "gq_ps", "z_ps"))
        qk_sb, glr_sb, cin_sb, gqk_sb, av_sb, ln_sb = (sem(n) for n in ("qk_sb", "glr_sb", "cin_sb", "gqk_sb", "av_sb", "ln_sb"))
        log_ready, e_ps, decay_sb, level_sb, s_ps, s_sb = (sem(n) for n in ("log_ready", "e_ps", "decay_sb", "level_sb", "s_ps", "s_sb"))
        att_ps, logits_sb, top_sb, exp_sb, prob_ready = (sem(n) for n in ("att_ps", "logits_sb", "top_sb", "exp_sb", "prob_ready"))
        pT_ps, pT_sb, atto_ps = sem("pT_ps"), sem("pT_sb"), sem("atto_ps")
        gv_ps, gv_sb, gr_ps, gr_sb, gr_silu = (sem(n) for n in ("gv_ps", "gv_sb", "gr_ps", "gr_sb", "gr_silu"))
        conv_sb, o_ps, sq8_sb, ms8_sb, rs8_sb, go_sb, go_ps, out_ps = (
            sem(n) for n in ("conv_sb", "o_ps", "sq8_sb", "ms8_sb", "rs8_sb", "go_sb", "go_ps", "out_ps"))
        mix_hi, mix_ready = sem("mix_hi"), sem("mix_ready")
        h1_ps, h3_ps, silu_sb, g_ready, gT_ps, gT_h, gT_ready, y_ps = (
            sem(n) for n in ("h1_ps", "h3_ps", "silu_sb", "g_ready", "gT_ps", "gT_h", "gT_ready", "y_ps"))
        logit_ps, gdiff_sb, gexp_sb, chosen_sb, place_ps, place_sb, count_sb, xn_h, xn_ready = (
            sem(n) for n in ("logit_ps", "gdiff_sb", "gexp_sb", "chosen_sb", "place_ps", "place_sb", "count_sb", "xn_h", "xn_ready"))
        e_silu, e_g, e_gT_ps, e_gT_h, e_gT = (
            sem(n) for n in ("e_silu", "e_g", "e_gT_ps", "e_gT_h", "e_gT"))
        pick_sb, xe_ps, xe_h, xe_ready, pickT_ps, pickT_sb = (
            sem(n) for n in ("pick_sb", "xe_ps", "xe_h", "xe_ready", "pickT_ps", "pickT_sb"))
        y_h, y_ready, back_ps, added = (sem(n) for n in ("y_h", "y_ready", "back_ps", "added"))
        rel_set = sem("rel_set")
        act_step, dve_step = sem("act_step"), sem("dve_step")
        stored = sem("stored")

        def ident():
            return consts[:, K_ID:K_ID + P]

        def lev(i):
            return consts[:, K_LEV + i * P:K_LEV + (i + 1) * P]

        def quarter(f, j, t):
            return f[:, 4 * j * SEQ:4 * (j + 1) * SEQ].rearrange("p (k s) -> p k s", k=4)[:, :, t * P:(t + 1) * P]

        def four(b):
            return b[:].rearrange("p (k s) -> p k s", k=4)

        block = ctx.enter_context(nc.Block())

        def expert_block(t, k):
            return t * PER_EXPERT + (MOE0 + k)

        def turned(c):
            return 2 * (c % 2) if c < CHUNKS - 1 else 2

        def hidden(engine, c, t, i, turn):
            if t == 0:
                engine.wait_ge((h1_ps, h3_ps)[i], turn + (c + 1))
            else:
                per = 2 if c < DENSE_FULL else 1
                engine.wait_ge(block_used, 6 * turn + (DENSE0 + 6 * c + per * (i + 1)))

        @block.sync
        def _(sp):
            def fill(n, src, rows, cols, turn=0, per=0, uses=0):
                s = raw_slot[n]
                before = n - SLOTS if n >= MOE0 + 4 or per == PER_EXPERT else raw_before[n]
                dst = raw[s][:, 0:rows * cols].rearrange("p (k c) -> p k c", k=rows)
                until = None if before is None else sp.lower_val(per * turn + before + 1)
                load = sp.dma_start(dst, src)
                if until is not None:
                    load.wait_op(lo_ready, until, "sem-ge")
                load.then_inc(raw_full[s], 16)

            def ktiles(w):
                return w.rearrange("(k p) c -> p k c", p=P)

            def mixer(l):
                b = BASE[l]
                w = ktiles(w_mix_in[l])
                for i, (c, nc_, k, nk) in enumerate(MIX_IN):
                    if l == 0 and i == 3:
                        sp.dma_start(consts[:, P:], consts_in[:, P:]).then_inc(tables_loaded, 16)
                    fill(b + i, w[:, k:k + nk, c:c + nc_], nk, nc_)
                wo = w_mix_out[l]
                for i, r in enumerate(OUT_ROWS):
                    fill(b + N_IN + i, ktiles(wo[r:r + 2 * P, :]), 2, D)

            def dense_chunk(c, turn):
                n = DENSE0 + 6 * c
                cols = ds(turn * FC + c * FC, FC)
                for i, w in enumerate((ffn_w1, ffn_w3)):
                    for k in range(2):
                        if c == 0 and i == 1 and k == 1:
                            sp.wait_ge(mix_ready, 4)
                        fill(n + 2 * i + k, ktiles(w[0])[:, 4 * k:4 * k + 4, cols], 4, FC, turn, 6)
                for k in range(2):
                    rows = ffn_w2[0][ds(turn * FC + (c * FC + 2 * P * k), 2 * P), :]
                    fill(n + 4 + k, ktiles(rows), 2, D, turn, 6)

            def expert(sweep, e, last=False, turn=0):
                n = MOE0
                t = EXPERTS * sweep + turn + e
                for c in range(1, CHUNKS):
                    for i in range(2):
                        fill_up(n + 6 * c - 2 + 2 * i, e, turn, t, c, i)
                    for k in range(2):
                        fill_w2(n + 6 * c + 2 + k, e, turn, t, c - 1, k)
                if not last:
                    fill_up(n + 40, e + 1, turn, t, 0, 0)
                for k in range(2):
                    fill_w2(n + (40 if last else 42) + k, e, turn, t, CHUNKS - 1, k)
                if not last:
                    fill_up(n + 44, e + 1, turn, t, 0, 1)

            def fill_up(n, e, turn, t, c, i):
                for k in range(2):
                    src = (moe_w1, moe_w3)[i][0].rearrange("e (k p) c -> p e k c", p=P)
                    src = src[:, ds(turn + e, 1), 4 * k:4 * k + 4, c * FC:(c + 1) * FC]
                    fill(n + k, src.rearrange("p e k c -> p (e k) c"), 4, FC, t, PER_EXPERT)

            def fill_w2(n, e, turn, t, c, k):
                src = moe_w2[0].rearrange("e (k p) c -> p e k c", p=P)
                src = src[:, ds(turn + e, 1), 4 * c + 2 * k:4 * c + 2 * k + 2, :]
                fill(n, src.rearrange("p e k c -> p (e k) c"), 2, D, t, PER_EXPERT)

            def sweep_experts(sweep):
                if sweep:
                    for i in range(2):
                        fill_up(MOE0 + 2 * i, 0, 0, EXPERTS * sweep, 0, i)
                with sp.Fori(0, EXPERTS - 1) as e:
                    expert(sweep, 0, turn=e)
                expert(sweep, EXPERTS - 1, last=True)

            for t in range(NT):
                sp.dma_start(x[:, t * D:(t + 1) * D], x_in[0, t * P:(t + 1) * P, :]).then_inc(x_loaded[t], 16)
                if t == 0:
                    row = g_mix[0]
                    sp.dma_start(g_row[:], bass.AP(tensor=row.tensor, offset=row.offset, ap=[[0, P], [1, D]])
                                 ).then_inc(first_gains, 16)
            sp.dma_start(consts[:, 0:P], consts_in[:, 0:P]).then_inc(consts_loaded, 16)
            mixer(0)
            dense_chunk(0, 0)
            dense_chunk(1, 0)
            with sp.Fori(0, DENSE_FULL - 3) as c:
                dense_chunk(2, c)
            dense_chunk(DENSE_FULL - 1, 0)
            n = DENSE0 + 6 * DENSE_FULL
            for i, w in enumerate((ffn_w1, ffn_w3)):
                fill(n + i, ktiles(w[0])[:, :, DENSE_FULL * FC:], KD, HALF)
            fill(n + 2, ktiles(ffn_w2[0][DENSE_FULL * FC:, :]), 2, D)
            mixer(1)
            for i, w in enumerate((moe_w1, moe_w3)):
                for k in range(2):
                    if i == 1 and k == 1:
                        sp.wait_ge(mix_ready, 8)
                    src = w[0][0].rearrange("(k p) c -> p k c", p=P)[:, 4 * k:4 * k + 4, 0:FC]
                    fill(MOE0 + 2 * i + k, src, 4, FC)
            sweep_experts(0)
            sp.wait_ge(count_sb, 1)
            count = sp.value_load(most_int[0:1, 0:1], min_val=0, max_val=SEQ)
            with sp.If(count > CAP):
                sweep_experts(1)
            for t in range(NT):
                sp.wait_ge(h_ready, 8 + t + 1)
                sp.dma_start(out[0, t * P:(t + 1) * P, :], h[:, t * D:(t + 1) * D]).then_inc(stored, 16)
            sp.wait_ge(stored, 16 * NT)

        @block.gpsimd
        def _(pool):
            def gains(row):
                pool.dma_start(g_row[:], bass.AP(tensor=row.tensor, offset=row.offset, ap=[[0, P], [1, D]])
                               ).then_inc(gains_loaded, 16)

            def gate_weights(l):
                g = w_gate[:, 0:256]
                pool.dma_start(g[0:RANK, :], gla_w_gate[l]).then_inc(gate_loaded, 16)
                pool.dma_start(g[RANK:RANK + 1, :], gla_b_gate[l:l + 1, :]).then_inc(gate_loaded, 16)

            def bias_tiles(l):
                for i, (tile_, n) in enumerate(((bias0, P), (bias1, 2 * P))):
                    src = bass.AP(tensor=bias_dram.tensor, offset=255 - P * i, ap=[[NH * 512 - 1, P], [512, NH], [1, n]])
                    pool.dma_start(tile_[:].rearrange("p (h s) -> p h s", h=NH), src).then_inc(bias_loaded, 16)

            def root(i):
                for t in range(NT):
                    pool.wait_ge(means, 2 * i + t + 1)
                    nc.gpsimd.tensor_tensor(rs[:, t:t + 1], ms[:, t:t + 1], power[:, 0:1], ALU.pow).then_inc(roots, 1)

            nc.gpsimd.memset(power, -0.5).then_inc(power_set, 1)
            pool.wait_ge(power_set, 1)
            pool.dma_start(setup_hot[0:REL_BUCKETS + 1, :], onehot_in).then_inc(hot_loaded, 16)
            pool.dma_start(setup_rel[0:REL_BUCKETS, 0:NH], rel_bias).then_inc(hot_loaded, 16)
            root(0)
            pool.dma_start(setup_masks[:], masks_in).then_inc(params_loaded, 16)
            pool.dma_start(conv_k, conv_w).then_inc(params_loaded, 16)
            pool.dma_start(gnorm, gla_g_norm).then_inc(params_loaded, 16)
            pool.dma_start(setup_router[:].rearrange("p (k e) -> p k e", k=KD),
                           moe_router[0].rearrange("(k p) e -> p k e", p=P)).then_inc(params_loaded, 16)
            pool.wait_ge(ones_set, 3)
            gate_weights(0)
            pool.wait_ge(bias_sb, NH)
            pool.dma_start(bias_dram, setup_bias[:]).then_inc(bias_stored, 16)
            pool.wait_ge(bias_stored, 16)
            bias_tiles(0)

            def head_roots(l):
                pool.wait_ge(ms8_sb, l + 1)
                nc.gpsimd.tensor_tensor(rs8, ms8, power, ALU.pow).then_inc(rs8_sb, 1)

            pool.wait_ge(power_set, 1)
            pool.wait_ge(h_ready, 2)
            gains(g_ffn[0])
            head_roots(0)
            root(1)
            pool.wait_ge(h_ready, 4)
            gains(g_mix[1])
            root(2)
            pool.wait_ge(x_ready, 4)
            pool.wait_ge(ones_set, 4)
            gate_weights(1)
            bias_tiles(1)
            pool.wait_ge(h_ready, 6)
            gains(g_ffn[1])
            head_roots(1)
            root(3)
            pool.wait_ge(h_ready, 8)
            gains(g_final)
            root(4)

        @block.scalar
        def _(act):
            def split(n, turn=0, per=0):
                s, w = raw_slot[n], n % SLOTS
                size = block_size(n)
                act.wait_ge(raw_full[s], 16 * (per // SLOTS) * turn + 16 * raw_use[n])
                if n >= SLOTS:
                    act.wait_ge(block_used, per * turn + n - SLOTS + 1)
                nc.scalar.copy(whi[w][:, 0:size], raw[s][:, 0:size]).then_inc(hi_ready, 1)

            def norm_squares(i, t):
                act.wait_ge(x_ready, 2 * (i - 1) + t + 1) if i else act.wait_ge(x_loaded[t], 16)
                nc.scalar.activation(h[:, t * D:(t + 1) * D], x[:, t * D:(t + 1) * D], ACT.Square,
                                     accum_out=sq[:, t:t + 1]).then_inc(squares, 1)

            def turn_hi(i, t):
                for j in range(2):
                    act.wait_ge(hT_ps, 4 * i + 2 * t + j + 1)
                    nc.scalar.copy(quarter(f_hi, j, t), four(bank[2 * t + j])).then_inc(hT_hi, 1)

            step = [0]

            def link(ins):
                step[0] += 1
                ins.then_inc(act_step, 1)
                act.wait_ge(act_step, step[0])

            def mixer(l):
                b = BASE[l]
                act.wait_ge(gr_ps, l + 1)
                nc.scalar.copy(gr[:, 0:512], bank[4][:]).then_inc(gr_sb, 1)
                act.wait_ge(block_used, b + 1)
                nc.scalar.copy(av[:], bank[5][:]).then_inc(av_sb, 1)
                split(b + 6)
                act.wait_ge(block_used, b + 3)
                nc.scalar.copy(gr[:, 512:1024], bank[6][:]).then_inc(gr_sb, 1)
                split(b + 7)
                split(b + 8)
                act.wait_ge(glr_ps, l + 1)
                act.wait_ge(ones_set, 3 + l)
                nc.scalar.copy(glr[0:RANK, :], bank[2][0:RANK, 0:256]).then_inc(glr_sb, 1)
                act.wait_ge(block_used, b + 5)
                nc.scalar.copy(cin[:], bank[3][:]).then_inc(cin_sb, 1)
                split(b + 9)
                split(b + 10)
                act.wait_ge(q_ps, l + 1)
                nc.scalar.copy(qT[:], bank[0][:]).then_inc(qk_sb, 1)
                act.wait_ge(block_used, b + 7)
                nc.scalar.copy(kT[:], bank[1][:]).then_inc(qk_sb, 1)
                split(b + 11)
                split(b + 12)
                act.wait_ge(z_ps, l + 1)
                link(nc.scalar.activation(z_a[:], bank[7][:], ACT.Abs))
                link(nc.scalar.activation(z_b[:], z_a[:], ACT.Exp, scale=-1.0))
                nc.scalar.activation(z_a[:], z_b[:], ACT.Ln, bias=1.0).then_inc(ln_sb, 1)
                act.wait_ge(gq_ps, l + 1)
                act.wait_ge(bias_stored, 16)
                nc.scalar.mul(gqT[:], bank[4][:], HD ** -0.5).then_inc(gqk_sb, 1)
                act.wait_ge(block_used, b + 9)
                nc.scalar.copy(gkT[:], bank[5][:]).then_inc(gqk_sb, 1)
                split(b + 13)
                split(b + 14)
                for t in range(NT):
                    act.wait_ge(top_sb, 2 * l + t + 1)
                    src, n = ((prob0, P), (prob1, 2 * P))[t]
                    for hh in range(NH):
                        c = NH * t + hh
                        ins = nc.scalar.activation(src[:, hh * n:(hh + 1) * n], src[:, hh * n:(hh + 1) * n], ACT.Exp,
                                                   bias=neg[:, c:c + 1], accum_out=rsum[:, c:c + 1])
                    ins.then_inc(exp_sb, 1)

                def level_decay(i):
                    act.wait_ge(e_ps, 8 * l + i + 1)
                    act.wait_ge(level_sb, 8 * l + i) if 8 * l + i else None
                    nc.scalar.activation(decay[:], bank[(4, 7)[i % 2]][:], ACT.Exp).then_inc(decay_sb, 1)

                level_decay(0)
                for t in range(NT):
                    act.wait_ge(gv_ps, l + 1) if t == 0 else act.wait_ge(block_used, b + 11)
                    nc.scalar.copy(gv[:, 512 * t:512 * (t + 1)], bank[5 + t][:]).then_inc(gv_sb, 1)
                level_decay(1)
                for j in range(3):
                    act.wait_ge(pT_ps, 3 * l + j + 1)
                    nc.scalar.copy(pT[:, 512 * j:512 * (j + 1)], bank[j][:]).then_inc(pT_sb, 1)
                split(b + 15)
                split(b + 16)
                for i in range(2, LEVELS + 1):
                    level_decay(i)
                    if i == 5:
                        act.wait_ge(block_used, b + 13)
                        act.wait_ge(atto_ps, l + 1)
                        nc.scalar.copy(f_hi[:, 0:512], bank[0][:]).then_inc(mix_hi, 1)
                    if i == 7:
                        act.wait_ge(conv_sb, l + 1)
                        nc.scalar.copy(f_hi[:, 512:1024], cy[:]).then_inc(mix_hi, 1)
                act.wait_ge(gr_sb, 2 * l + 2)
                nc.scalar.activation(gr[:], gr[:], ACT.Silu).then_inc(gr_silu, 1)
                split(b + 17)
                split(b + 18)
                for t in range(NT):
                    act.wait_ge(o_ps, 2 * l + t + 1)
                    for hh in range(NH):
                        c = NH * t + hh
                        ins = nc.scalar.activation((decay, log_a)[t][:, hh * P:(hh + 1) * P], bank[3 + t][:, hh * P:(hh + 1) * P], ACT.Square,
                                                   accum_out=sq8[:, c:c + 1])
                ins.then_inc(sq8_sb, 1)
                for j in range(2):
                    act.wait_ge(go_ps, 2 * l + j + 1)
                    nc.scalar.activation(f_hi[:, 1024 + 512 * j:1536 + 512 * j], bank[5 + j][:], ACT.Copy,
                                         scale=gnorm[:, l:l + 1]).then_inc(mix_hi, 1)
                split(b + 19)
                norm_squares(2 * l + 1, 0)
                turn_hi(2 * l + 1, 0)
                norm_squares(2 * l + 1, 1)
                if l == 0:
                    split(b + 20)
                turn_hi(2 * l + 1, 1)
                if l:
                    split(b + 20)

            def d_silu(c, t, turn=0, width=FC):
                hidden(act, c, t, 0, turn)
                nc.scalar.activation(gate_out[t][:, 0:width], bank[2 * t][:, 0:width], ACT.Silu).then_inc(silu_sb, 1)

            def d_gT(c, t, turn=0, width=FC):
                act.wait_ge(gT_ps, 2 * turn + 2 * c + t + 1)
                nc.scalar.copy(gT_hi[t][:, 0:width], bank[2 * t][:, 0:width]).then_inc(gT_h, 1)

            def dense_chunk(c, turn=0):
                n = DENSE0 + 6 * c
                width = FC if c < DENSE_FULL else HALF
                if c:
                    d_silu(c - 1, 1, turn)
                    d_gT(c - 1, 1, turn)
                d_silu(c, 0, turn, width)
                if c < DENSE_FULL:
                    for k in range(2):
                        split(n + 4 + k, turn, 6)
                    d_gT(c, 0, turn)
                    for k in range(4 if c < DENSE_FULL - 1 else 2):
                        split(n + 6 + k, turn, 6)
                else:
                    split(n + 2)
                    d_gT(c, 0, 0, width)
                    split(BASE[1])
                    d_silu(c, 1, 0, width)
                    d_gT(c, 1, 0, width)
                    norm_squares(2, 0)
                    turn_hi(2, 0)
                    split(BASE[1] + 1)
                    norm_squares(2, 1)
                    split(BASE[1] + 2)
                    turn_hi(2, 1)
                    split(BASE[1] + 3)
                    split(BASE[1] + 4)
                    split(BASE[1] + 5)

            def e_silu_(c, t):
                act.wait_ge(block_used, expert_block(t, 6 * c if c else 2))
                nc.scalar.activation(gate_out[c % 2][:], bank[2 * (c % 2)][:], ACT.Silu).then_inc(e_silu, 1)

            def e_gT_hi_(c, u):
                act.wait_ge(e_gT_ps, u + c + 1)
                nc.scalar.copy(e_gT_hi[:], bank[turned(c)][:]).then_inc(e_gT_h, 1)

            def gathered(v):
                for j in range(2):
                    act.wait_ge(xe_ps, v + j + 1)
                    nc.scalar.copy(xe_hi[:, 512 * j:512 * (j + 1)], bank[6 + j][:]).then_inc(xe_h, 1)

            def pick_turned(v):
                act.wait_ge(pickT_ps, v + 1)
                nc.scalar.copy(pickT[:], bank[3][:, 0:NT * P]).then_inc(pickT_sb, 1)

            def expert(sweep, e, turn=0, last=False):
                t = turn + (EXPERTS * sweep + e)
                u = t * CHUNKS

                def sp_(k):
                    split(MOE0 + k, t, PER_EXPERT)

                for c in range(1, CHUNKS):
                    if c > 1:
                        e_silu_(c - 1, t)
                    sp_(6 * c + 2)
                    sp_(6 * c + 3)
                    e_gT_hi_(c - 1, u)
                    if c < CHUNKS - 1:
                        for k in range(4):
                            sp_(6 * c + 4 + k)
                e_silu_(CHUNKS - 1, t)
                sp_(40)
                sp_(41)
                if not last:
                    act.wait_ge(block_used, expert_block(t, 38))
                    gathered(t * 2 + 2)
                e_gT_hi_(CHUNKS - 1, u)
                if not last:
                    for k in range(42, 46):
                        sp_(k)
                for j in range(2):
                    act.wait_ge(block_used, expert_block(t, 42 if last else 44))
                    nc.scalar.copy(y_hi[:, 512 * j:512 * (j + 1)], bank[4 + j][:]).then_inc(y_h, 1)
                if not last:
                    sp_(46)
                    sp_(47)
                    e_silu_(0, t + 1)
                    sp_(48)
                    sp_(49)
                    pick_turned(t + 1)

            def sweep_experts(sweep):
                if sweep:
                    for k in range(4):
                        split(MOE0 + k, EXPERTS * sweep, PER_EXPERT)
                gathered(2 * EXPERTS * sweep)
                pick_turned(EXPERTS * sweep)
                if sweep:
                    for k in range(4, 6):
                        split(MOE0 + k, EXPERTS * sweep, PER_EXPERT)
                e_silu_(0, EXPERTS * sweep)
                for k in range(6, 8):
                    split(MOE0 + k, EXPERTS * sweep, PER_EXPERT)
                with act.Fori(0, EXPERTS - 1) as e:
                    expert(sweep, 0, turn=e)
                expert(sweep, EXPERTS - 1, last=True)

            for t in range(NT):
                norm_squares(0, t)
            turn_hi(0, 0)
            split(0)
            turn_hi(0, 1)
            split(1)
            split(2)
            act.wait_ge(params_loaded, 64)
            nc.scalar.copy(router_hi[:], setup_router[:]).then_inc(router_split, 1)
            for k in range(3, 6):
                split(k)
            mixer(0)
            dense_chunk(0)
            dense_chunk(1)
            with act.Fori(0, DENSE_FULL - 3) as c:
                dense_chunk(2, c)
            dense_chunk(DENSE_FULL - 1)
            dense_chunk(DENSE_FULL)
            mixer(1)
            split(MOE0 + 4)
            split(MOE0 + 5)
            act.wait_ge(logit_ps, 1)
            for t in range(NT):
                nc.scalar.copy(xn_hi[:, t * D:(t + 1) * D], h[:, t * D:(t + 1) * D]).then_inc(xn_h, 1)
            act.wait_ge(gdiff_sb, 1)
            nc.scalar.activation(gexp, gdiff, ACT.Exp).then_inc(gexp_sb, 1)
            sweep_experts(0)
            act.wait_ge(count_sb, 1)
            count = act.value_load(most_int[0:1, 0:1], min_val=0, max_val=SEQ)
            with act.If(count > CAP):
                sweep_experts(1)
            for t in range(NT):
                norm_squares(4, t)

        @block.vector
        def _(dve):
            step = [0]

            def link(ins):
                step[0] += 1
                ins.then_inc(dve_step, 1)
                dve.wait_ge(dve_step, step[0])

            def split(n, turn=0, per=0):
                s, w = raw_slot[n], n % SLOTS
                size = block_size(n)
                dve.wait_ge(hi_ready, per * turn + n + 1)
                nc.vector.tensor_tensor(wlo[w][:, 0:size], raw[s][:, 0:size], whi[w][:, 0:size].bitcast(F32),
                                        ALU.subtract).then_inc(lo_ready, 1)

            def rest(dst, src, hi, sem_in, value, sem_out):
                dve.wait_ge(sem_in, value)
                nc.vector.tensor_tensor(dst, src, hi.bitcast(F32), ALU.subtract).then_inc(sem_out, 1)

            def norm_row(i, t):
                dve.wait_ge(squares, 2 * i + t + 1)
                nc.vector.tensor_scalar(ms[:, t:t + 1], sq[:, t:t + 1], 1.0 / D, EPS, ALU.mult, ALU.add).then_inc(means, 1)
                dve.wait_ge(roots, 2 * i + t + 1)
                dve.wait_ge(gains_loaded, 16 * i) if i else dve.wait_ge(first_gains, 16)
                nc.vector.scalar_tensor_tensor(h[:, t * D:(t + 1) * D], x[:, t * D:(t + 1) * D], rs[:, t:t + 1],
                                               g_row[:], ALU.mult, ALU.mult).then_inc(h_ready, 1)

            def turn_lo(i, t):
                for j in range(2):
                    rest(quarter(f_lo, j, t), four(bank[2 * t + j]), quarter(f_hi, j, t),
                         hT_hi, 4 * i + 2 * t + j + 1, hT_ready)

            def norm(i, t):
                norm_row(i, t)
                turn_lo(i, t)

            def ones_row(l):
                nc.vector.memset(glr[0:32, :], 1.0).then_inc(ones_set, 1)

            def mixer(l):
                b = BASE[l]
                for k in range(6, 13):
                    split(b + k)
                dve.wait_ge(ln_sb, l + 1)
                dve.wait_ge(bias_stored, 16)
                link(nc.vector.scalar_tensor_tensor(log_a[:], bank[7][:], 0.0, z_a[:], ALU.min, ALU.subtract))
                nc.vector.tensor_scalar(log_a[:], log_a[:], 1.0 / 16.0, None, ALU.mult).then_inc(log_ready, 1)
                split(b + 13)
                split(b + 14)
                dve.wait_ge(bias_loaded, 32 * (l + 1))
                for t in range(NT):
                    n = P * (t + 1)
                    dst = (prob0, prob1)[t][:].rearrange("p (a o s) -> p a o s", a=2, o=2)
                    bias = (bias0, bias1)[t][:].rearrange("p (a o s) -> p a o s", a=2, o=2)
                    for odd in range(2):
                        dve.wait_ge(att_ps, 4 * l + 2 * t + odd + 1)
                        src = bank[((0, 3), (1, 2))[t][odd]][:, 0:2 * n].rearrange("p (a s) -> p a s", a=2)
                        ins = nc.vector.scalar_tensor_tensor(dst[:, :, odd, :], src, HD ** -0.5, bias[:, :, odd, :],
                                                             ALU.mult, ALU.add)
                        ins.then_inc(logits_sb, 1)
                    dve.wait_ge(logits_sb, 4 * l + 2 * t + 2)
                    link(nc.vector.tensor_reduce(top[:, NH * t:NH * (t + 1)],
                                                 (prob0, prob1)[t][:].rearrange("p (h s) -> p h s", h=NH), AX, ALU.max))
                    nc.vector.tensor_scalar(neg[:, NH * t:NH * (t + 1)], top[:, NH * t:NH * (t + 1)], -1.0, None,
                                            ALU.mult).then_inc(top_sb, 1)
                for t in range(NT):
                    n = P * (t + 1)
                    dve.wait_ge(exp_sb, 2 * l + t + 1)
                    link(nc.vector.reciprocal(rinv[:, NH * t:NH * (t + 1)], rsum[:, NH * t:NH * (t + 1)]))
                    src = (prob0, prob1)[t]
                    for hh in range(NH):
                        c = NH * t + hh
                        ins = nc.vector.tensor_scalar(src[:, hh * n:(hh + 1) * n], src[:, hh * n:(hh + 1) * n],
                                                      rinv[:, c:c + 1], None, ALU.mult)
                    ins.then_inc(prob_ready, 1)

                def level_operands(i):
                    dve.wait_ge(decay_sb, 8 * l + i + 1)
                    if i >= 2:
                        dve.wait_ge(s_ps, 2 * (9 * l + i))
                    off = 1024 * (i % 2)
                    nc.vector.tensor_tensor(qk_level[:, off:off + 512], gqT[:], decay[:], ALU.mult)
                    nc.vector.tensor_tensor(qk_level[:, off + 512:off + 1024], gkT[:], decay[:],
                                            ALU.mult).then_inc(level_sb, 1)

                def level_scores(i):
                    for odd in range(2):
                        v = 18 * l + 2 * (i + 1) + odd + 1
                        dve.wait_ge(s_ps, v)
                        if i == LEVELS:
                            nc.vector.tensor_copy(cross[:, 256 * odd:256 * (odd + 1)],
                                                  bank[5 + odd][:, 0:256]).then_inc(s_sb, 1)
                            continue
                        dst = scores[:, 512 * odd:512 * (odd + 1)].rearrange("p (g t) -> p g t", g=4)
                        src = bank[5 + odd][:].rearrange("p (g t) -> p g t", g=4)
                        if i < 0:
                            one = ident().rearrange("p (g t) -> p g t", g=1).broadcast_to([P, 4, P])
                            nc.vector.tensor_tensor(dst, src, one, ALU.mult).then_inc(s_sb, 1)
                        else:
                            dve.wait_ge(s_sb, v - 2)
                            m = masks[:, i * P:(i + 1) * P].rearrange("p (g t) -> p g t", g=1).broadcast_to([P, 4, P])
                            nc.vector.copy_predicated(dst, m, src).then_inc(s_sb, 1)

                dve.wait_ge(gqk_sb, 2 * l + 2)
                level_operands(0)
                level_operands(1)
                dve.wait_ge(masks_set, 1)
                dve.wait_ge(consts_loaded, 16)
                dve.wait_ge(tables_loaded, 16)
                level_scores(-1)
                for i in range(LEVELS + 1):
                    level_scores(i)
                    if i + 2 <= LEVELS:
                        level_operands(i + 2)
                    if i == 0:
                        split(b + 15)
                        split(b + 16)
                    if i == 5:
                        dve.wait_ge(block_used, b + 13)
                        nc.vector.tensor_tensor(cy[:], cy[:], bank[1][:], ALU.mult).then_inc(conv_sb, 1)
                        rest(f_lo[:, 0:512], bank[0][:], f_hi[:, 0:512], mix_hi, 4 * l + 1, mix_ready)
                    if i == 7:
                        rest(f_lo[:, 512:1024], cy[:], f_hi[:, 512:1024], mix_hi, 4 * l + 2, mix_ready)
                    if i == 3:
                        dve.wait_ge(c_ps, l + 1)
                        dve.wait_ge(cin_sb, l + 1)
                        link(nc.vector.tensor_tensor(cin[:], cin[:], bank[2][:], ALU.mult))
                        w = conv_k[:, 6 * l:6 * l + 6]
                        for half in range(2):
                            o = 256 * half
                            ins = nc.vector.tensor_scalar(cy[:, o:o + 256], cin[:, o:o + 256],
                                                          w[:, 3 * half + 2:3 * half + 3], None, ALU.mult)
                        link(ins)
                        for back in (1, 2):
                            for half in range(2):
                                o = 256 * half
                                ins = nc.vector.scalar_tensor_tensor(
                                    cy[:, o + back:o + 256], cin[:, o:o + 256 - back],
                                    w[:, 3 * half + 2 - back:3 * half + 3 - back], cy[:, o + back:o + 256],
                                    ALU.mult, ALU.add)
                            link(ins)
                split(b + 17)
                split(b + 18)
                dve.wait_ge(sq8_sb, l + 1)
                nc.vector.tensor_scalar(ms8, sq8, 1.0 / DV, EPS, ALU.mult, ALU.add).then_inc(ms8_sb, 1)
                dve.wait_ge(rs8_sb, l + 1)
                dve.wait_ge(gr_silu, l + 1)
                for t in range(NT):
                    for hh in range(NH):
                        c = NH * t + hh
                        ins = nc.vector.scalar_tensor_tensor(
                            go[:, c * P:(c + 1) * P], bank[3 + t][:, hh * P:(hh + 1) * P], rs8[:, c:c + 1],
                            gr[:, c * P:(c + 1) * P], ALU.mult, ALU.mult)
                ins.then_inc(go_sb, 1)
                for j in range(2):
                    dve.wait_ge(mix_hi, 4 * l + 3 + j)
                    o = 1024 + 512 * j
                    nc.vector.scalar_tensor_tensor(f_lo[:, o:o + 512], bank[5 + j][:], gnorm[:, l:l + 1],
                                                   f_hi[:, o:o + 512].bitcast(F32), ALU.mult,
                                                   ALU.subtract).then_inc(mix_ready, 1)
                split(b + 19)
                for t in range(NT):
                    dve.wait_ge(block_used, b + N_MIX) if t else dve.wait_ge(out_ps, l + 1)
                    for j in range(2):
                        o = D * t + 512 * j
                        ins = nc.vector.tensor_tensor(x[:, o:o + 512], x[:, o:o + 512], bank[(0, 1, 2, 7)[2 * t + j]][:],
                                                      ALU.add)
                    ins.then_inc(x_ready, 1)
                    if t and l == 0:
                        split(b + 20)
                    norm(2 * l + 1, t)
                if l:
                    split(b + 20)

            def d_mult(c, t, turn=0, width=FC):
                u = 2 * c + t
                dve.wait_ge(silu_sb, 2 * turn + u + 1)
                hidden(dve, c, t, 1, turn)
                nc.vector.tensor_tensor(gate_out[t][:, 0:width], gate_out[t][:, 0:width], bank[2 * t + 1][:, 0:width],
                                        ALU.mult).then_inc(g_ready, 1)

            def d_gT(c, t, turn=0, width=FC):
                u = 2 * c + t
                rest(gT_lo[t][:, 0:width], bank[2 * t][:, 0:width], gT_hi[t][:, 0:width],
                     gT_h, 2 * turn + u + 1, gT_ready)

            def dense_chunk(c, turn=0):
                n = DENSE0 + 6 * c
                width = FC if c < DENSE_FULL else HALF
                if c:
                    d_mult(c - 1, 1, turn)
                    d_gT(c - 1, 1, turn)
                d_mult(c, 0, turn, width)
                if c < DENSE_FULL:
                    for k in range(2):
                        split(n + 4 + k, turn, 6)
                    d_gT(c, 0, turn)
                    for k in range(4 if c < DENSE_FULL - 1 else 2):
                        split(n + 6 + k, turn, 6)
                else:
                    split(n + 2)
                    d_gT(c, 0, 0, width)
                    split(BASE[1])
                    d_mult(c, 1, 0, width)
                    d_gT(c, 1, 0, width)
                    for t in range(NT):
                        dve.wait_ge(y_ps, c + 1) if t == 0 else dve.wait_ge(block_used, BASE[1])
                        for j in range(2):
                            o = D * t + 512 * j
                            ins = nc.vector.tensor_tensor(x[:, o:o + 512], x[:, o:o + 512], bank[4 + 2 * t + j][:],
                                                          ALU.add)
                        ins.then_inc(x_ready, 1)
                        if t == 0:
                            norm_row(2, 0)
                    turn_lo(2, 0)
                    split(BASE[1] + 1)
                    norm_row(2, 1)
                    split(BASE[1] + 2)
                    turn_lo(2, 1)
                    split(BASE[1] + 3)
                    split(BASE[1] + 4)
                    split(BASE[1] + 5)

            def picks0():
                for t in range(NT):
                    nc.vector.tensor_scalar(pick[:, t * P:(t + 1) * P], consts[:, K_IOTA:K_IOTA + P],
                                            place1[:, EXPERTS * t:EXPERTS * t + 1], None,
                                            ALU.is_equal).then_inc(pick_sb, 1)

            def route():
                dve.wait_ge(logit_ps, 1)
                link(nc.vector.tensor_copy(logit, bank[4][:, 0:16]))
                down = consts[:, K_DOWN:K_DOWN + EXPERTS]
                for src, m, r, hot in ((logit, m1, r1, hot1), (second, m2, r2, hot2)):
                    if src is second:
                        link(nc.vector.scalar_tensor_tensor(second, hot1, -3.0e38, logit, ALU.mult, ALU.add))
                    link(nc.vector.tensor_reduce(m, src.rearrange("p (t e) -> p t e", t=NT), AX, ALU.max))
                    for t in range(NT):
                        o = EXPERTS * t
                        ins = nc.vector.scalar_tensor_tensor(key[:, o:o + EXPERTS], src[:, o:o + EXPERTS], m[:, t:t + 1],
                                                             down, ALU.is_equal, ALU.mult)
                        if t == 0:
                            ins.then_inc(dve_step, 1)
                            step[0] += 1
                    link(ins)
                    link(nc.vector.tensor_reduce(r, key.rearrange("p (t e) -> p t e", t=NT), AX, ALU.max))
                    for t in range(NT):
                        o = EXPERTS * t
                        link(nc.vector.tensor_scalar(hot[:, o:o + EXPERTS], down, r[:, t:t + 1], None, ALU.is_equal))
                nc.vector.tensor_tensor(gdiff, m2, m1, ALU.subtract).then_inc(gdiff_sb, 1)
                nc.vector.tensor_tensor(chosen, hot1, hot2, ALU.add).then_inc(chosen_sb, 1)
                for t in range(NT):
                    o = t * D
                    rest(xn_lo[:, o:o + D], h[:, o:o + D], xn_hi[:, o:o + D], xn_h, t + 1, xn_ready)
                dve.wait_ge(place_ps, 1)
                dve.wait_ge(chosen_sb, 1)
                link(nc.vector.tensor_tensor(place1, chosen, bank[5][:, 0:16], ALU.mult))
                link(nc.vector.tensor_scalar(place1, place1, -1.0, None, ALU.add))
                picks0()
                link(nc.vector.tensor_reduce(most, bank[5][:, 16:24], AX, ALU.max))
                link(nc.vector.tensor_scalar(place2, place1, -float(CAP), None, ALU.add))
                nc.vector.tensor_copy(most_int[:, 0:1], most).then_inc(count_sb, 1)
                dve.wait_ge(gexp_sb, 1)
                link(nc.vector.tensor_scalar(g1, gexp, 1.0, None, ALU.add))
                link(nc.vector.reciprocal(g1, g1))
                link(nc.vector.tensor_tensor(g2, gexp, g1, ALU.mult))
                for t in range(NT):
                    o = EXPERTS * t
                    link(nc.vector.tensor_scalar(hot2[:, o:o + EXPERTS], hot2[:, o:o + EXPERTS], g2[:, t:t + 1], None,
                                                 ALU.mult))
                for t in range(NT):
                    o = EXPERTS * t
                    link(nc.vector.scalar_tensor_tensor(gates[:, o:o + EXPERTS], hot1[:, o:o + EXPERTS], g1[:, t:t + 1],
                                                        hot2[:, o:o + EXPERTS], ALU.mult, ALU.add))
                nc.vector.memset(small2[:, 54:55], 0.0).then_inc(added, 1)

            def picks(sweep, e, v):
                dve.wait_ge(pickT_ps, v)
                where = (place1, place2)[sweep]
                for t in range(NT):
                    nc.vector.tensor_scalar(pick[:, t * P:(t + 1) * P], consts[:, K_IOTA:K_IOTA + P],
                                            where[:, ds(e + EXPERTS * t, 1)], None, ALU.is_equal).then_inc(pick_sb, 1)

            def gathered(v):
                for j in range(2):
                    rest(xe_lo[:, 512 * j:512 * (j + 1)], bank[6 + j][:], xe_hi[:, 512 * j:512 * (j + 1)],
                         xe_h, v + j + 1, xe_ready)

            def e_mult(c, u, t):
                dve.wait_ge(e_silu, u + c + 1)
                dve.wait_ge(block_used, expert_block(t, 6 * c + 2 if c else 4))
                nc.vector.tensor_tensor(gate_out[c % 2][:], gate_out[c % 2][:], bank[2 * (c % 2) + 1][:],
                                        ALU.mult).then_inc(e_g, 1)

            def e_gT_rest(c, u):
                rest(e_gT_lo[:], bank[turned(c)][:], e_gT_hi[:], e_gT_h, u + c + 1, e_gT)

            def expert(sweep, e, turn=0, last=False):
                t_ = turn + (EXPERTS * sweep + e)
                u = t_ * CHUNKS

                def sp_(k):
                    split(MOE0 + k, t_, PER_EXPERT)

                for c in range(1, CHUNKS):
                    if c > 1:
                        e_mult(c - 1, u, t_)
                    sp_(6 * c + 2)
                    sp_(6 * c + 3)
                    e_gT_rest(c - 1, u)
                    if c == 3 and not last:
                        picks(sweep, turn + (e + 1), t_ + 1)
                    if c < CHUNKS - 1:
                        for k in range(4):
                            sp_(6 * c + 4 + k)
                sp_(40)
                sp_(41)
                e_mult(CHUNKS - 1, u, t_)
                if not last:
                    gathered(t_ * 2 + 2)
                e_gT_rest(CHUNKS - 1, u)
                if not last:
                    for k in range(42, 46):
                        sp_(k)
                for j in range(2):
                    rest(y_lo[:, 512 * j:512 * (j + 1)], bank[4 + j][:], y_hi[:, 512 * j:512 * (j + 1)],
                         y_h, t_ * 2 + j + 1, y_ready)
                if not last:
                    sp_(46)
                    sp_(47)
                    e_mult(0, u + CHUNKS, t_ + 1)
                    sp_(48)
                    sp_(49)
                for t in range(NT):
                    for j in range(2):
                        dve.wait_ge(back_ps, t_ * 4 + (2 * t + j + 1))
                        o = D * t + 512 * j
                        nxt = nc.vector.scalar_tensor_tensor(x[:, o:o + 512], bank[(6, 4)[t] + j][:],
                                                       gates[:, ds(turn + (e + EXPERTS * t), 1)], x[:, o:o + 512],
                                                       ALU.mult, ALU.add)
                nxt.then_inc(added, 1)
                dve.wait_ge(added, t_ + 2)

            def sweep_experts(sweep):
                if sweep:
                    for k in range(4):
                        split(MOE0 + k, EXPERTS * sweep, PER_EXPERT)
                    picks(sweep, 0, EXPERTS * sweep)
                gathered(2 * EXPERTS * sweep)
                if sweep:
                    for k in range(4, 6):
                        split(MOE0 + k, EXPERTS * sweep, PER_EXPERT)
                for k in range(6, 8):
                    split(MOE0 + k, EXPERTS * sweep, PER_EXPERT)
                e_mult(0, EXPERTS * sweep * CHUNKS, EXPERTS * sweep)
                with dve.Fori(0, EXPERTS - 1) as e:
                    expert(sweep, 0, turn=e)
                expert(sweep, EXPERTS - 1, last=True)

            nc.vector.memset(ones[:], 1.0).then_inc(ones_set, 1)
            nc.vector.memset(w_gate[0:32, :], 0.0).then_inc(ones_set, 1)
            ones_row(0)
            nc.vector.memset(setup_wide[REL_BUCKETS:REL_BUCKETS + 1, :], 1.0).then_inc(rel_set, 1)
            for t in range(NT):
                norm_row(0, t)
            dve.wait_ge(hot_loaded, 32)
            nc.vector.tensor_copy(setup_wide[0:REL_BUCKETS, :].rearrange("p (h m) -> p h m", h=NH),
                                  setup_rel[0:REL_BUCKETS, 0:NH].rearrange("p (h m) -> p h m", m=1)
                                  .broadcast_to([REL_BUCKETS, NH, P])).then_inc(rel_set, 1)
            turn_lo(0, 0)
            split(0)
            turn_lo(0, 1)
            split(1)
            split(2)
            for i in range(NH):
                dve.wait_ge(bias_ps, i + 1)
                nc.vector.tensor_copy(setup_bias[:, 512 * i:512 * (i + 1)],
                                      bank[(0, 1, 2, 7)[i]][:]).then_inc(bias_sb, 1)
            dve.wait_ge(router_split, 1)
            nc.vector.tensor_tensor(router_lo[:], setup_router[:], router_hi[:].bitcast(F32),
                                    ALU.subtract).then_inc(router_split, 1)
            for k in range(3, 6):
                split(k)
            dve.wait_ge(params_loaded, 64)
            nc.vector.tensor_copy(masks[:], setup_masks[:]).then_inc(masks_set, 1)
            mixer(0)
            dense_chunk(0)
            dense_chunk(1)
            with dve.Fori(0, DENSE_FULL - 3) as c:
                dense_chunk(2, c)
            dense_chunk(DENSE_FULL - 1)
            dense_chunk(DENSE_FULL)
            dve.wait_ge(x_ready, 4)
            ones_row(1)
            mixer(1)
            split(MOE0 + 4)
            route()
            split(MOE0 + 5)
            sweep_experts(0)
            dve.wait_ge(count_sb, 1)
            count = dve.value_load(most_int[0:1, 0:1], min_val=0, max_val=SEQ)
            with dve.If(count > CAP):
                sweep_experts(1)
            for t in range(NT):
                nc.vector.tensor_copy(small2[:, 52 + t:53 + t], x[:, t * D:t * D + 1]).then_inc(x_ready, 1)
            for t in range(NT):
                norm_row(4, t)

        @block.tensor
        def _(pe):
            mm = nc.tensor.matmul

            def split3(dst, a_hi, a_lo, b_hi, b_lo, start, stop):
                mm(dst, a_hi, b_hi, start=start, stop=False)
                mm(dst, a_hi, b_lo, start=False, stop=False)
                return mm(dst, a_lo, b_hi, start=False, stop=stop)

            def weights(n, k, cols, c0, c1):
                w = n % SLOTS
                return (whi[w][:, k * cols + c0:k * cols + c1], wlo[w][:, k * cols + c0:k * cols + c1])

            def rows(k, t):
                o = k * SEQ + t * P
                return f_hi[:, o:o + P], f_lo[:, o:o + P]

            def feats(k):
                return f_hi[:, k * SEQ:(k + 1) * SEQ], f_lo[:, k * SEQ:(k + 1) * SEQ]

            def turn_rows(i, t):
                pe.wait_ge(h_ready, 2 * i + t + 1)
                for k in range(KD):
                    ins = pe.transpose(bank[2 * t + k // 4][:, k % 4 * P:(k % 4 + 1) * P],
                                       h[:, t * D + k * P:t * D + (k + 1) * P], ident())
                    if k % 4 == 3:
                        ins.then_inc(hT_ps, 1)

            def by_feature(blocks, cols, outs, free=True):
                ks = [(n, k) for n, nk in blocks for k in range(nk)]
                pe.wait_ge(lo_ready, blocks[-1][0] + 1)
                for i, (bk, at_, c, signal) in enumerate(outs):
                    for j, (n, k) in enumerate(ks):
                        w_hi, w_lo = weights(n, k, cols, c, c + P)
                        f_h, f_l = feats(j)
                        ins = split3(bank[bk][:, at_:at_ + SEQ], w_hi, w_lo, f_h, f_l, j == 0, j == len(ks) - 1)
                        if free and i == len(outs) - 1 and k == dict(blocks)[n] - 1:
                            ins.then_inc(block_used, 1)
                    if signal is not None:
                        ins.then_inc(signal, 1)

            def by_token(blocks, cols, t, bk, at_, signal):
                ks = [(n, k) for n, nk in blocks for k in range(nk)]
                pe.wait_ge(lo_ready, blocks[-1][0] + 1)
                for j, (n, k) in enumerate(ks):
                    w_hi, w_lo = weights(n, k, cols, 0, cols)
                    f_h, f_l = rows(j, t)
                    ins = split3(bank[bk][:, at_:at_ + cols], f_h, f_l, w_hi, w_lo, j == 0, j == len(ks) - 1)
                    if t == NT - 1 and k == dict(blocks)[n] - 1:
                        ins.then_inc(block_used, 1)
                if t == 0 and signal is not None:
                    ins.then_inc(signal, 1)

            def keep_warm(n):
                for _ in range(n):
                    mm(bank[6][:, 0:256], ident(), consts[:, 0:256], start=True, stop=True)

            def bias_by_distance():
                pe.wait_ge(hot_loaded, 32)
                pe.wait_ge(rel_set, 2)
                for i in range(NH):
                    mm(bank[(0, 1, 2, 7)[i]][:], setup_wide[0:REL_BUCKETS + 1, i * P:(i + 1) * P],
                       setup_hot[0:REL_BUCKETS + 1, :], start=True, stop=True).then_inc(bias_ps, 1)

            def head(i):
                return 64 * (i % 2), i // 2

            def mixer(l):
                b = BASE[l]
                for t in range(NT):
                    if l and t:
                        turn_rows(2, t)
                    pe.wait_ge(hT_ready, 8 * l + 2 * t + 2)
                    if l == 0 and t == 1:
                        bias_by_distance()
                    by_token([(b, 8)], 256, t, 5, 256 * t, None)
                    by_token([(b + 1, 4), (b + 2, 4)], 512, t, (4, 6)[t], 0, gr_ps)
                pe.wait_ge(bias_sb, NH)
                by_feature([(b + 3, 4), (b + 4, 4)], 272,
                           [(2, 0, 0, glr_ps), (3, 0, RANK, None), (3, SEQ, RANK + P, None)])
                by_feature([(b + 5, 4), (b + 6, 4)], 512,
                           [(0, 0, 0, None), (0, SEQ, P, q_ps), (1, 0, 2 * P, None), (1, SEQ, 3 * P, None)])
                pe.wait_ge(glr_sb, l + 1)
                pe.wait_ge(gate_loaded, 32 * (l + 1))
                for t in range(NT):
                    ins = mm(bank[7][:, 256 * t:256 * (t + 1)], glr[0:32, t * P:(t + 1) * P], w_gate[0:32, 0:256],
                             start=True, stop=True)
                ins.then_inc(z_ps, 1)
                pe.wait_ge(gr_sb, 2 * l + 2)
                pe.wait_ge(av_sb, l + 1)
                by_feature([(b + 7, 4), (b + 8, 4)], 512,
                           [(4, 0, 0, None), (4, SEQ, P, gq_ps), (5, 0, 2 * P, None), (5, SEQ, 3 * P, None)])
                pe.wait_ge(qk_sb, 2 * l + 2)
                pe.wait_ge(cin_sb, l + 1)
                for t in range(NT):
                    n = P * (t + 1)
                    for i in range(NH):
                        off, pr = head(i)
                        bk = ((0, 3), (1, 2))[t][i % 2]
                        ins = mm(bank[bk][:, pr * n:(pr + 1) * n], qT[off:off + HD, pr * SEQ + t * P:pr * SEQ + (t + 1) * P],
                                 kT[off:off + HD, pr * SEQ:pr * SEQ + n], start=True, stop=True)
                        if pr == 1:
                            ins.then_inc(att_ps, 1)

                def decay_sums(i):
                    for pr in range(2):
                        for t in range(NT):
                            m = lev(i) if i < LEVELS else lev(LEVELS + t)
                            ins = mm(bank[(4, 7)[i % 2]][:, pr * SEQ + t * P:pr * SEQ + (t + 1) * P],
                                     log_a[:, t * 256 + pr * P:t * 256 + (pr + 1) * P], m, start=True, stop=True)
                    ins.then_inc(e_ps, 1)

                pe.wait_ge(log_ready, l + 1)
                pe.wait_ge(tables_loaded, 16)
                pe.wait_ge(gqk_sb, 2 * l + 2)
                decay_sums(0)
                decay_sums(1)
                pe.wait_ge(av_sb, l + 1)
                for t in range(NT):
                    by_token([(b + 9, 4), (b + 10, 4)], 512, t, 5 + t, 0, gv_ps)
                for t in range(NT):
                    pe.wait_ge(prob_ready, 2 * l + t + 1)
                    for s in range(t + 1):
                        for i in range(NH):
                            n = P * (t + 1)
                            ins = pe.transpose(bank[t + s][:, i * P:(i + 1) * P],
                                               (prob0, prob1)[t][:, i * n + s * P:i * n + (s + 1) * P], ident())
                        ins.then_inc(pT_ps, 1)

                def level(i):
                    if i < 0:
                        q, k = gqT[:], gkT[:]
                        pe.wait_ge(gv_sb, 2 * l + 2)
                    else:
                        off_ = 1024 * (i % 2)
                        q, k = qk_level[:, off_:off_ + 512], qk_level[:, off_ + 512:off_ + 1024]
                        pe.wait_ge(level_sb, 8 * l + i + 1)
                        pe.wait_ge(s_sb, 18 * l + 2 * (i + 1))
                    for pr in range(2):
                        for t in range(NT if i < LEVELS else 1):
                            for odd in range(2):
                                off = 64 * odd
                                g = pr * NT + t if i < LEVELS else pr
                                tq = t if i < LEVELS else 1
                                o = pr * SEQ
                                ins = mm(bank[5 + odd][:, g * P:(g + 1) * P],
                                         k[off:off + HD, o + t * P:o + (t + 1) * P],
                                         q[off:off + HD, o + tq * P:o + (tq + 1) * P], start=True, stop=True)
                                if g == (3 if i < LEVELS else 1):
                                    ins.then_inc(s_ps, 1)

                def project(j, t):
                    n = b + N_IN + j
                    pe.wait_ge(mix_ready, 4 * l + j + 1)
                    pe.wait_ge(lo_ready, n + 1)
                    for k in range(2):
                        for half in range(2):
                            w_hi, w_lo = weights(n, k, D, 512 * half, 512 * (half + 1))
                            f_h, f_l = rows(2 * j + k, t)
                            ins = split3(bank[(0, 1, 2, 7)[2 * t + half]][:], f_h, f_l, w_hi, w_lo,
                                         j == 0 and k == 0, j == 3 and k == 1)
                    if t:
                        ins.then_inc(block_used, 1)
                    elif j == 3:
                        ins.then_inc(out_ps, 1)

                level(-1)
                level(0)
                decay_sums(2)
                pe.wait_ge(pT_sb, 3 * l + 3)
                for i in range(NH):
                    off, pr = head(i)

                    def values(s):
                        return av[:, s * 256 + i * HD:s * 256 + (i + 1) * HD]

                    o = bank[0][off:off + HD, pr * SEQ:(pr + 1) * SEQ]
                    mm(o[:, 0:P], values(0), pT[:, i * P:(i + 1) * P], start=True, stop=True)
                    mm(o[:, P:SEQ], values(0), pT[:, 512 + i * P:512 + (i + 1) * P], start=True, stop=False)
                    ins = mm(o[:, P:SEQ], values(1), pT[:, 1024 + i * P:1024 + (i + 1) * P], start=False, stop=True)
                ins.then_inc(atto_ps, 1)

                conv_gates = [(b + 11, 4), (b + 12, 4)]
                for i in range(LEVELS + 1):
                    if i:
                        level(i)
                    if i and i + 2 <= LEVELS:
                        decay_sums(i + 2)
                    if i == 0:
                        by_feature(conv_gates, 512, [(2, 0, 2 * P, None), (2, SEQ, 3 * P, c_ps)], free=False)
                    if i == 4:
                        by_feature(conv_gates, 512, [(1, 0, 0, None), (1, SEQ, P, None)])
                    if i == 6:
                        pe.wait_ge(conv_sb, l + 1)
                        project(0, 0)
                pe.wait_ge(s_sb, 18 * (l + 1))
                for t in range(NT):
                    for i in range(NH):
                        odd, pr = i % 2, i // 2
                        o = bank[3 + t][:, i * P:(i + 1) * P]

                        def inside(s):
                            a = 512 * odd + (pr * NT + s) * P
                            return scores[:, a:a + P]

                        if t:
                            mm(o, cross[:, 256 * odd + pr * P:256 * odd + (pr + 1) * P], gv[:, i * DV:(i + 1) * DV],
                               start=True, stop=False)
                        ins = mm(o, inside(t), gv[:, t * 512 + i * DV:t * 512 + (i + 1) * DV], start=t == 0, stop=True)
                    ins.then_inc(o_ps, 1)
                pe.wait_ge(decay_sb, 8 * (l + 1))
                project(0, 1)
                project(1, 0)
                pe.wait_ge(go_sb, l + 1)
                for j in range(2):
                    for q in range(4):
                        i, t = 2 * j + q // 2, q % 2
                        ins = pe.transpose(bank[5 + j][:, q * P:(q + 1) * P],
                                           go[:, (NH * t + i) * P:(NH * t + i + 1) * P], ident())
                    ins.then_inc(go_ps, 1)
                project(1, 1)
                project(2, 0)
                project(3, 0)
                project(2, 1)
                project(3, 1)

            def up(bk, f, blocks, width, waits, signal):
                for s, v in waits:
                    pe.wait_ge(s, v)
                j = 0
                total = sum(nk for _, nk, _ in blocks)
                for w, nk, v in blocks:
                    pe.wait_ge(lo_ready, v)
                    for k in range(nk):
                        f_h, f_l = f(j)
                        w_hi, w_lo = (x_[w][:, k * width:(k + 1) * width] for x_ in (whi, wlo))
                        ins = split3(bank[bk][:, 0:width], f_h, f_l, w_hi, w_lo, j == 0, j == total - 1)
                        j += 1
                    if signal is None:
                        ins.then_inc(block_used, 1)
                if signal is not None:
                    ins.then_inc(signal, 1)

            def turn_gate(src, bk, width, ready, v, signal):
                pe.wait_ge(ready, v)
                for q in range(width // P):
                    ins = pe.transpose(bank[bk][:, q * P:(q + 1) * P], src[:, q * P:(q + 1) * P], ident())
                ins.then_inc(signal, 1)

            def down(y0, g_h, g_l, blocks, first, final, ready, v, signal):
                pe.wait_ge(ready, v)
                k0 = 0
                for i, (w, v_) in enumerate(blocks):
                    pe.wait_ge(lo_ready, v_)
                    for k in range(2):
                        for half in range(2):
                            o = k * D + 512 * half
                            ins = split3(bank[y0 + half][:], g_h[:, k0 * P:(k0 + 1) * P], g_l[:, k0 * P:(k0 + 1) * P],
                                         whi[w][:, o:o + 512], wlo[w][:, o:o + 512],
                                         first and k0 == 0, final and i == len(blocks) - 1 and k == 1)
                        k0 += 1
                    if signal is None:
                        ins.then_inc(block_used, 1)
                if signal is not None:
                    ins.then_inc(signal, 1)

            def dense_up(c, t, i, turn=0):
                n = DENSE0 + 6 * c + 2 * i
                if c < DENSE_FULL:
                    blocks = [((n + k) % SLOTS, 4, 6 * turn + n + k + 1) for k in range(2)]
                    width = FC
                else:
                    n = DENSE0 + 6 * c + i
                    blocks = [(n % SLOTS, 8, n + 1)]
                    width = HALF
                up(2 * t + i, lambda j: rows(j, t), blocks, width, [], (h1_ps, h3_ps)[i] if t == 0 else None)

            def dense_turn(c, t, turn=0):
                turn_gate(gate_out[t], 2 * t, FC if c < DENSE_FULL else HALF, g_ready, 2 * turn + 2 * c + t + 1, gT_ps)

            def dense_down(c, t, turn=0):
                n = DENSE0 + 6 * c + 4
                if c < DENSE_FULL:
                    blocks = [((n + k) % SLOTS, 6 * turn + n + k + 1) for k in range(2)]
                else:
                    n = DENSE0 + 6 * c + 2
                    blocks = [(n % SLOTS, n + 1)]
                down(4 + 2 * t, gT_hi[t], gT_lo[t], blocks, c == 0, c == DENSE_FULL, gT_ready,
                     2 * turn + 2 * c + t + 1, y_ps if t == 0 else None)

            def dense_chunk(c, turn=0):
                if c == 0:
                    turn_rows(1, 0)
                    pe.wait_ge(hT_ready, 6)
                dense_up(c, 0, 0, turn)
                if c:
                    dense_turn(c - 1, 1, turn)
                dense_up(c, 0, 1, turn)
                if c:
                    dense_down(c - 1, 1, turn)
                else:
                    turn_rows(1, 1)
                    pe.wait_ge(hT_ready, 8)
                dense_up(c, 1, 0, turn)
                dense_turn(c, 0, turn)
                dense_up(c, 1, 1, turn)
                dense_down(c, 0, turn)

            def gather(v):
                pe.wait_ge(pick_sb, v * 2 + 2)
                for k in range(KD):
                    o = bank[6 + k // 4][:, (k % 4) * P:(k % 4 + 1) * P]
                    for t in range(NT):
                        a = t * D + k * P
                        mm(o, xn_hi[:, a:a + P], pick[:, t * P:(t + 1) * P], start=t == 0, stop=False)
                        ins = mm(o, xn_lo[:, a:a + P], pick[:, t * P:(t + 1) * P], start=False, stop=t == NT - 1)
                    if k % 4 == 3:
                        ins.then_inc(xe_ps, 1)

            def turn_pick():
                for t in range(NT):
                    ins = pe.transpose(bank[3][:, t * P:(t + 1) * P], pick[:, t * P:(t + 1) * P].bitcast(F32), ident())
                ins.then_inc(pickT_ps, 1)

            def expert(sweep, e, turn=0, last=False, first=False):
                t_ = turn + (EXPERTS * sweep + e)
                u = t_ * CHUNKS
                nb = t_ * PER_EXPERT

                def places(k):
                    return xe_hi[:, k * P:(k + 1) * P], xe_lo[:, k * P:(k + 1) * P]

                def pair(k):
                    return [((MOE0 + k + i) % SLOTS, nb + (MOE0 + k + i + 1)) for i in range(2)]

                def e_up(c, i, k, ahead=0):
                    waits = []
                    if c == 0 and i == 0:
                        waits.append((xe_ready, (t_ + ahead) * 2 + 2))
                    if c == 1 and i == 1:
                        waits.append((pickT_sb, t_ + 1))
                    up(2 * (c % 2) + i, places, [(w, 4, v) for w, v in pair(k)], FC, waits, None)

                def e_turn(c):
                    turn_gate(gate_out[c % 2], turned(c), FC, e_g, u + c + 1, e_gT_ps)

                def e_down(c, k):
                    if c == 0:
                        pe.wait_ge(added, t_ + 1)
                    down(4, e_gT_hi, e_gT_lo, pair(k), c == 0, c == CHUNKS - 1, e_gT, u + c + 1, None)

                if first:
                    e_up(0, 0, 0)
                    e_up(0, 1, 2)
                    return
                for c in range(1, CHUNKS):
                    e_up(c, 0, 6 * c - 2)
                    e_turn(c - 1)
                    if c == CHUNKS - 1 and not last:
                        gather(t_ + 1)
                    e_up(c, 1, 6 * c)
                    e_down(c - 1, 6 * c + 2)
                e_turn(CHUNKS - 1)
                if not last:
                    e_up(0, 0, 40, ahead=1)
                e_down(CHUNKS - 1, 40 if last else 42)
                if not last:
                    e_up(0, 1, 44)
                pe.wait_ge(y_ready, t_ * 2 + 2)
                for t in range(NT):
                    for j in range(2):
                        o = bank[(6, 4)[t] + j][:]
                        mm(o, pickT[:, t * P:(t + 1) * P], y_hi[:, 512 * j:512 * (j + 1)], start=True, stop=False)
                        mm(o, pickT[:, t * P:(t + 1) * P], y_lo[:, 512 * j:512 * (j + 1)], start=False,
                           stop=True).then_inc(back_ps, 1)
                if not last:
                    turn_pick()

            def sweep_experts(sweep):
                if sweep:
                    pe.wait_ge(added, EXPERTS * sweep + 1)
                gather(EXPERTS * sweep)
                turn_pick()
                expert(sweep, 0, first=True)
                with pe.Fori(0, EXPERTS - 1) as e:
                    expert(sweep, 0, turn=e)
                expert(sweep, EXPERTS - 1, last=True)

            pe.wait_ge(consts_loaded, 16)
            for t in range(NT):
                turn_rows(0, t)
            mixer(0)
            dense_chunk(0)
            dense_chunk(1)
            with pe.Fori(0, DENSE_FULL - 3) as c:
                dense_chunk(2, c)
            dense_chunk(DENSE_FULL - 1)
            dense_chunk(DENSE_FULL)
            dense_turn(DENSE_FULL, 1)
            dense_down(DENSE_FULL, 1)
            turn_rows(2, 0)
            mixer(1)
            pe.wait_ge(router_split, 2)
            for t in range(NT):
                turn_rows(3, t)
                pe.wait_ge(hT_ready, 12 + 2 * t + 2)
                for k in range(KD):
                    f_h, f_l = rows(k, t)
                    ins = split3(bank[4][:, 8 * t:8 * t + 8], f_h, f_l, router_hi[:, 8 * k:8 * k + 8],
                                 router_lo[:, 8 * k:8 * k + 8], k == 0, k == KD - 1)
            ins.then_inc(logit_ps, 1)
            keep_warm(6)
            pe.wait_ge(chosen_sb, 1)
            until = lev(LEVELS + 1)
            mm(bank[5][:, 0:8], until, chosen[:, 0:8], start=True, stop=True)
            mm(bank[5][:, 8:16], ones[:], chosen[:, 0:8], start=True, stop=False)
            mm(bank[5][:, 8:16], until, chosen[:, 8:16], start=False, stop=True)
            mm(bank[5][:, 16:24], ones[:], chosen[:, 0:8], start=True, stop=False)
            mm(bank[5][:, 16:24], ones[:], chosen[:, 8:16], start=False, stop=True).then_inc(place_ps, 1)
            keep_warm(2)
            pe.wait_ge(xn_ready, 2)
            sweep_experts(0)
            pe.wait_ge(count_sb, 1)
            count = pe.value_load(most_int[0:1, 0:1], min_val=0, max_val=SEQ)
            with pe.If(count > CAP):
                sweep_experts(1)


_OUT_SHAPE = (1, SEQ, D)


def kernel(x, w_mix_in, w_mix_out, g_mix, rel_bias, gla_w_gate, gla_b_gate, gla_g_norm, conv_w, g_ffn,
           ffn_w1, ffn_w3, ffn_w2, moe_router, moe_w1, moe_w3, moe_w2, g_final):
    import concourse.bacc as bacc
    from concourse.bass_utils import run_bass_kernel_spmd

    given = dict(x=x, w_mix_in=w_mix_in, w_mix_out=w_mix_out, g_mix=g_mix, rel_bias=rel_bias, gla_w_gate=gla_w_gate,
                 gla_b_gate=gla_b_gate, gla_g_norm=gla_g_norm, conv_w=conv_w, g_ffn=g_ffn, ffn_w1=ffn_w1,
                 ffn_w3=ffn_w3, ffn_w2=ffn_w2, moe_router=moe_router, moe_w1=moe_w1, moe_w3=moe_w3, moe_w2=moe_w2,
                 g_final=g_final)
    taps = np.asarray(conv_w).reshape(DEPTH, 3, 2, P).transpose(3, 0, 2, 1).reshape(P, DEPTH * 6)
    given.update(conv_w=taps, gla_g_norm=np.asarray(gla_g_norm).T)
    c, m, o = shape_constants()
    given.update(shape_consts=c, shape_masks=m, shape_buckets=o)
    nc = bacc.Bacc("TRN2", target_bir_lowering=False, num_devices=1)
    arrays, args = {}, []
    for name, a in given.items():
        a = np.ascontiguousarray(a)
        arrays[f"in_{name}"] = a
        args.append(nc.dram_tensor(f"in_{name}", a.shape, mybir.dt.from_np(a.dtype), kind="ExternalInput").ap())
    args.append(nc.dram_tensor("out_0", _OUT_SHAPE, F32, kind="ExternalOutput").ap())
    trunk(nc, *args)
    r = run_bass_kernel_spmd(nc, [arrays], core_ids=[0])
    return r.results[0]["out_0"]
```
